# Optimizing a Trainium2 kernel written in Bass

```python
import math
import jax, jax.numpy as jnp
from jax import lax
import numpy as np

D_MODEL = 1024
BATCH = 1
SEQ = 1024
DEPTH = 2
DEC_BATCH = 8
DEC_SEQ = 1
PAST_LEN = 8192
PAGE_SIZE = 128

N_EVEN = (DEPTH + 1) // 2
N_ODD = DEPTH // 2
CHUNK = 64
EPS = 1e-6
NEG = -1e30
A_HEADS = 4
A_DK = 128
A_DV = 128
CONV_W = 4
A_QK = A_HEADS * A_DK
A_V = A_HEADS * A_DV
A_CONV_CH = 2 * A_QK + A_V
B_HEADS = 4
B_DK = 128
B_DV = 128
B_QK = B_HEADS * B_DK
B_V = B_HEADS * B_DV
ROPE_BASE = 10000.0
IN_A = A_CONV_CH + 2 * A_HEADS + A_V + 2 * B_QK + 2 * B_V
MIX_A = A_V + B_V
C_HEADS = 4
C_DK = 128
C_DV = 256
C_QK = C_HEADS * C_DK
C_V = C_HEADS * C_DV
IN_C = 2 * C_QK + 2 * C_V + 2 * C_HEADS
D_FF = 4 * D_MODEL

kernel_name = 'hybrid_gdn_retention_mlstm_step'

def rmsnorm(x, g):
    xf = x.astype(jnp.float32)
    y = xf * lax.rsqrt(jnp.mean(xf * xf, axis=-1, keepdims=True) + EPS)
    return (y * g.astype(jnp.float32)).astype(x.dtype)

def _l2norm(t):
    return t * lax.rsqrt(jnp.sum(t * t, axis=-1, keepdims=True) + EPS)

def _heads(t, h):
    b, l, _ = t.shape
    return t.reshape(b, l, h, -1).transpose(0, 2, 1, 3)

def _merge(t):
    b, h, l, d = t.shape
    return t.transpose(0, 2, 1, 3).reshape(b, l, h * d)

def _rope(t, pos):
    half = t.shape[-1] // 2
    inv = ROPE_BASE ** (-jnp.arange(half, dtype=jnp.float32) / half)
    ang = pos.astype(jnp.float32)[:, None] * inv[None, :]
    cos, sin = jnp.cos(ang), jnp.sin(ang)
    t1, t2 = t[..., :half], t[..., half:]
    return jnp.concatenate([t1 * cos - t2 * sin, t1 * sin + t2 * cos], axis=-1)

def causal_conv(u, buf, w):
    l = u.shape[1]
    xp = jnp.concatenate([buf, u], axis=1)
    out = sum(xp[:, i:i + l] * w[i] for i in range(CONV_W))
    return out, xp[:, -(CONV_W - 1):]

def _chunk_layout(l):
    c = min(CHUNK, l)
    n = -(-l // c)
    return c, n, n * c - l

def _to_chunks(t, c, n, pad, pad_value=0.0):
    widths = [(0, 0), (0, 0), (0, pad)] + [(0, 0)] * (t.ndim - 3)
    t = jnp.pad(t, widths, constant_values=pad_value)
    t = t.reshape(t.shape[:2] + (n, c) + t.shape[3:])
    return jnp.moveaxis(t, 2, 0)

def _from_chunks(o, l):
    o = jnp.moveaxis(o, 0, 2)
    o = o.reshape(o.shape[:2] + (-1,) + o.shape[4:])
    return o[:, :, :l]

def _masks(c):
    idx = jnp.arange(c)
    return idx[:, None] > idx[None, :], idx[:, None] >= idx[None, :]

def gated_delta_rule(q, k, v, beta, log_a, s0):
    l = q.shape[2]
    c, n, pad = _chunk_layout(l)
    q, k, v, beta, log_a = (_to_chunks(t, c, n, pad) for t in (q, k, v, beta, log_a))
    strict, causal = _masks(c)
    g = jnp.cumsum(log_a, axis=-1)
    diff = g[..., :, None] - g[..., None, :]
    decay_strict = jnp.exp(jnp.where(strict, diff, -jnp.inf))
    decay_causal = jnp.exp(jnp.where(causal, diff, -jnp.inf))
    kb = k * beta[..., None]
    lower = jnp.einsum('nbhik,nbhjk->nbhij', kb, k) * decay_strict
    a_mat = lower + jnp.eye(c, dtype=lower.dtype)
    dv = v.shape[-1]
    rhs = jnp.concatenate([v * beta[..., None], kb * jnp.exp(g)[..., None]], axis=-1)
    sol = lax.linalg.triangular_solve(a_mat, rhs, left_side=True, lower=True)
    u, w = sol[..., :dv], sol[..., dv:]
    qk = jnp.einsum('nbhik,nbhjk->nbhij', q, k) * decay_causal
    q_dec = q * jnp.exp(g)[..., None]
    k_dec = k * jnp.exp(g[..., -1:] - g)[..., None]
    g_last = jnp.exp(g[..., -1])

    def step(s, xs):
        u_c, w_c, qk_c, qd_c, kd_c, gl_c = xs
        v_new = u_c - jnp.einsum('bhik,bhkv->bhiv', w_c, s)
        o = jnp.einsum('bhik,bhkv->bhiv', qd_c, s) + jnp.einsum('bhij,bhjv->bhiv', qk_c, v_new)
        s = s * gl_c[..., None, None] + jnp.einsum('bhjk,bhjv->bhkv', kd_c, v_new)
        return s, o

    s, o = lax.scan(step, s0, (u, w, qk, q_dec, k_dec, g_last))
    return _from_chunks(o, l), s

def decayed_linear_attention(q, k, v, log_a, s0):
    l = q.shape[2]
    c, n, pad = _chunk_layout(l)
    q, k, v, log_a = (_to_chunks(t, c, n, pad) for t in (q, k, v, log_a))
    _, causal = _masks(c)
    g = jnp.cumsum(log_a, axis=-1)
    diff = g[..., :, None] - g[..., None, :]
    decay_causal = jnp.exp(jnp.where(causal, diff, -jnp.inf))
    qk = jnp.einsum('nbhik,nbhjk->nbhij', q, k) * decay_causal
    q_dec = q * jnp.exp(g)[..., None]
    k_dec = k * jnp.exp(g[..., -1:] - g)[..., None]
    g_last = jnp.exp(g[..., -1])

    def step(s, xs):
        qk_c, qd_c, kd_c, v_c, gl_c = xs
        o = jnp.einsum('bhik,bhkv->bhiv', qd_c, s) + jnp.einsum('bhij,bhjv->bhiv', qk_c, v_c)
        s = s * gl_c[..., None, None] + jnp.einsum('bhjk,bhjv->bhkv', kd_c, v_c)
        return s, o

    s, o = lax.scan(step, s0, (qk, q_dec, k_dec, v, g_last))
    return _from_chunks(o, l), s

def mlstm_chunkwise(q, k, v, i_pre, log_f, c0, n0, m0):
    l = q.shape[2]
    c, n, pad = _chunk_layout(l)
    q, k, v, log_f = (_to_chunks(t, c, n, pad) for t in (q, k, v, log_f))
    i_pre = _to_chunks(i_pre, c, n, pad, NEG)
    _, causal = _masks(c)
    b = jnp.cumsum(log_f, axis=-1)
    d_log = jnp.where(causal, b[..., :, None] - b[..., None, :] + i_pre[..., None, :], NEG)
    d_max = jnp.max(d_log, axis=-1)
    qk = jnp.einsum('nbhik,nbhjk->nbhij', q, k)
    k_log = b[..., -1:] - b + i_pre

    def step(carry, xs):
        cm, nv, m = carry
        q_c, k_c, v_c, b_c, dl_c, dm_c, qk_c, kl_c = xs
        inter = b_c + m[..., None]
        m_row = jnp.maximum(inter, dm_c)
        w_intra = jnp.exp(dl_c - m_row[..., None]) * qk_c
        w_inter = jnp.exp(inter - m_row)
        num = w_inter[..., None] * jnp.einsum('bhik,bhkv->bhiv', q_c, cm) + jnp.einsum('bhij,bhjv->bhiv', w_intra, v_c)
        den = w_inter * jnp.einsum('bhik,bhk->bhi', q_c, nv) + jnp.sum(w_intra, axis=-1)
        h = num / jnp.maximum(jnp.abs(den), jnp.exp(-m_row))[..., None]
        m_new = m_row[..., -1]
        f_state = jnp.exp(b_c[..., -1] + m - m_new)
        kw = k_c * jnp.exp(kl_c - m_new[..., None])[..., None]
        cm = cm * f_state[..., None, None] + jnp.einsum('bhjk,bhjv->bhkv', kw, v_c)
        nv = nv * f_state[..., None] + jnp.sum(kw, axis=-2)
        return (cm, nv, m_new), h

    (cm, nv, m), h = lax.scan(step, (c0, n0, m0), (q, k, v, b, d_log, d_max, qk, k_log))
    return _from_chunks(h, l), cm, nv, m

def mixer_ab(xn, pos, conv_buf, s_delta, s_ret, w_in, w_conv, a_log, dt_bias, gdn_gain, ret_gain, w_out):
    f32 = jnp.float32
    proj = (xn @ w_in).astype(f32)
    cuts = np.cumsum([A_CONV_CH, A_HEADS, A_HEADS, A_V, B_QK, B_QK, B_V]).tolist()
    qkv_a, a_raw, b_raw, g_a, q_b, k_b, v_b, g_b = jnp.split(proj, cuts, axis=-1)
    conv_out, new_buf = causal_conv(qkv_a, conv_buf.astype(f32), w_conv.astype(f32))
    conv_out = jax.nn.silu(conv_out)
    q_a, k_a, v_a = jnp.split(conv_out, [A_QK, 2 * A_QK], axis=-1)
    q_a = _l2norm(_heads(q_a, A_HEADS)) * A_DK ** -0.5
    k_a = _l2norm(_heads(k_a, A_HEADS))
    v_a = _heads(v_a, A_HEADS)
    beta = jax.nn.sigmoid(b_raw).transpose(0, 2, 1)
    log_alpha = (-jnp.exp(a_log.astype(f32)) * jax.nn.softplus(a_raw + dt_bias.astype(f32))).transpose(0, 2, 1)
    o_a, s_delta_new = gated_delta_rule(q_a, k_a, v_a, beta, log_alpha, s_delta.astype(f32))
    o_a = rmsnorm(o_a, gdn_gain) * jax.nn.silu(_heads(g_a, A_HEADS))
    q_b = _rope(_heads(q_b, B_HEADS), pos)
    k_b = _rope(_heads(k_b, B_HEADS), pos) * B_DK ** -0.5
    v_b = _heads(v_b, B_HEADS)
    log_gamma = jnp.log1p(-jnp.exp2(-5.0 - jnp.arange(B_HEADS, dtype=f32)))
    log_gamma = jnp.broadcast_to(log_gamma[None, :, None], q_b.shape[:3])
    o_b, s_ret_new = decayed_linear_attention(q_b, k_b, v_b, log_gamma, s_ret.astype(f32))
    o_b = rmsnorm(o_b, ret_gain) * jax.nn.silu(_heads(g_b, B_HEADS))
    mixed = jnp.concatenate([_merge(o_a), _merge(o_b)], axis=-1).astype(xn.dtype)
    return mixed @ w_out, new_buf, s_delta_new, s_ret_new

def mixer_c(xn, s_c, s_n, s_m, w_in, b_gate, mlstm_gain, w_out):
    f32 = jnp.float32
    proj = (xn @ w_in).astype(f32)
    q, k, v, o_pre, gates = jnp.split(proj, np.cumsum([C_QK, C_QK, C_V, C_V]).tolist(), axis=-1)
    gates = (gates + b_gate.astype(f32)).transpose(0, 2, 1)
    i_pre, f_pre = gates[:, :C_HEADS], gates[:, C_HEADS:]
    h, cm, nv, m = mlstm_chunkwise(_heads(q, C_HEADS), _heads(k, C_HEADS) * C_DK ** -0.5, _heads(v, C_HEADS),
                                   i_pre, jax.nn.log_sigmoid(f_pre), s_c.astype(f32), s_n.astype(f32), s_m.astype(f32))
    h = rmsnorm(h, mlstm_gain) * jax.nn.sigmoid(_heads(o_pre, C_HEADS))
    return _merge(h).astype(xn.dtype) @ w_out, cm, nv, m

def squared_relu_mlp(xn, w_up, w_down):
    hid = jax.nn.relu(xn @ w_up)
    return (hid * hid) @ w_down

def run_group(x, pos, conv_a, delta_a, ret_b, m_c, m_n, m_m, p):
    h = x
    new_conv, new_delta, new_ret, new_c, new_n, new_m = [], [], [], [], [], []
    for layer in range(DEPTH):
        i = layer // 2
        if layer % 2 == 0:
            xn = rmsnorm(h, p['norm_mix_a'][i])
            mix, cb, sd, sr = mixer_ab(xn, pos, conv_a[i], delta_a[i], ret_b[i], p['w_in_a'][i], p['w_conv_a'][i],
                                       p['a_log'][i], p['dt_bias'][i], p['gdn_gain'][i], p['ret_gain'][i], p['w_out_a'][i])
            new_conv.append(cb)
            new_delta.append(sd)
            new_ret.append(sr)
        else:
            xn = rmsnorm(h, p['norm_mix_c'][i])
            mix, cm, nv, m = mixer_c(xn, m_c[i], m_n[i], m_m[i], p['w_in_c'][i], p['b_gate_c'][i],
                                     p['mlstm_gain'][i], p['w_out_c'][i])
            new_c.append(cm)
            new_n.append(nv)
            new_m.append(m)
        h = h + mix
        h = h + squared_relu_mlp(rmsnorm(h, p['norm_ffn'][layer]), p['w_up'][layer], p['w_down'][layer])
    y = rmsnorm(h, p['final_gain'])
    return (y, jnp.stack(new_conv), jnp.stack(new_delta), jnp.stack(new_ret),
            jnp.stack(new_c), jnp.stack(new_n), jnp.stack(new_m))

def setup_inputs(seed: int = 0) -> dict:
    key = jax.random.key(seed)
    ks = list(jax.random.split(key, 32))
    f32 = jnp.float32

    def nrm(k, shape, scale):
        return jax.random.normal(k, shape, f32) * scale

    dt = jnp.exp(jax.random.uniform(ks[20], (N_EVEN, A_HEADS), f32, math.log(1e-3), math.log(1e-1)))
    dt_bias = dt + jnp.log(-jnp.expm1(-dt))
    a_log = jnp.log(jax.random.uniform(ks[21], (N_EVEN, A_HEADS), f32, 1.0, 16.0))
    b_gate = jnp.concatenate([nrm(ks[22], (N_ODD, C_HEADS), 0.1),
                              jax.random.uniform(ks[23], (N_ODD, C_HEADS), f32, 3.0, 6.0)], axis=-1)
    return {
        'x_prompt': nrm(ks[0], (BATCH, SEQ, D_MODEL), 1.0),
        'x_sample': nrm(ks[1], (DEC_BATCH, DEC_SEQ, D_MODEL), 1.0),
        'state_conv_a': nrm(ks[2], (N_EVEN, DEC_BATCH, CONV_W - 1, A_CONV_CH), 1.0),
        'state_delta_a': nrm(ks[3], (N_EVEN, DEC_BATCH, A_HEADS, A_DK, A_DV), 0.5),
        'state_ret_b': nrm(ks[4], (N_EVEN, DEC_BATCH, B_HEADS, B_DK, B_DV), 1.0),
        'state_mlstm_C': nrm(ks[5], (N_ODD, DEC_BATCH, C_HEADS, C_DK, C_DV), 0.5),
        'state_mlstm_n': nrm(ks[6], (N_ODD, DEC_BATCH, C_HEADS, C_DK), 0.5),
        'state_mlstm_m': nrm(ks[7], (N_ODD, DEC_BATCH, C_HEADS), 1.0),
        'norm_mix_a': 1.0 + nrm(ks[8], (N_EVEN, D_MODEL), 0.02),
        'w_in_a': nrm(ks[9], (N_EVEN, D_MODEL, IN_A), D_MODEL ** -0.5),
        'w_conv_a': nrm(ks[10], (N_EVEN, CONV_W, A_CONV_CH), CONV_W ** -0.5),
        'a_log': a_log,
        'dt_bias': dt_bias,
        'gdn_gain': 1.0 + nrm(ks[11], (N_EVEN, A_DV), 0.02),
        'ret_gain': 1.0 + nrm(ks[12], (N_EVEN, B_DV), 0.02),
        'w_out_a': nrm(ks[13], (N_EVEN, MIX_A, D_MODEL), MIX_A ** -0.5),
        'norm_mix_c': 1.0 + nrm(ks[14], (N_ODD, D_MODEL), 0.02),
        'w_in_c': nrm(ks[15], (N_ODD, D_MODEL, IN_C), D_MODEL ** -0.5),
        'b_gate_c': b_gate,
        'mlstm_gain': 1.0 + nrm(ks[16], (N_ODD, C_DV), 0.02),
        'w_out_c': nrm(ks[17], (N_ODD, C_V, D_MODEL), C_V ** -0.5),
        'norm_ffn': 1.0 + nrm(ks[18], (DEPTH, D_MODEL), 0.02),
        'w_up': nrm(ks[19], (DEPTH, D_MODEL, D_FF), D_MODEL ** -0.5),
        'w_down': nrm(ks[24], (DEPTH, D_FF, D_MODEL), D_FF ** -0.5),
        'final_gain': 1.0 + nrm(ks[25], (D_MODEL,), 0.02),
    }

def reference(x_prompt, x_sample, state_conv_a, state_delta_a, state_ret_b, state_mlstm_C, state_mlstm_n, state_mlstm_m,
              norm_mix_a, w_in_a, w_conv_a, a_log, dt_bias, gdn_gain, ret_gain, w_out_a,
              norm_mix_c, w_in_c, b_gate_c, mlstm_gain, w_out_c, norm_ffn, w_up, w_down, final_gain):
    p = dict(norm_mix_a=norm_mix_a, w_in_a=w_in_a, w_conv_a=w_conv_a, a_log=a_log, dt_bias=dt_bias,
             gdn_gain=gdn_gain, ret_gain=ret_gain, w_out_a=w_out_a, norm_mix_c=norm_mix_c, w_in_c=w_in_c,
             b_gate_c=b_gate_c, mlstm_gain=mlstm_gain, w_out_c=w_out_c, norm_ffn=norm_ffn, w_up=w_up,
             w_down=w_down, final_gain=final_gain)
    f32 = jnp.float32
    bp = x_prompt.shape[0]
    z_conv = jnp.zeros((N_EVEN, bp, CONV_W - 1, A_CONV_CH), f32)
    z_delta = jnp.zeros((N_EVEN, bp, A_HEADS, A_DK, A_DV), f32)
    z_ret = jnp.zeros((N_EVEN, bp, B_HEADS, B_DK, B_DV), f32)
    z_c = jnp.zeros((N_ODD, bp, C_HEADS, C_DK, C_DV), f32)
    z_n = jnp.zeros((N_ODD, bp, C_HEADS, C_DK), f32)
    z_m = jnp.zeros((N_ODD, bp, C_HEADS), f32)
    pos_prompt = jnp.arange(x_prompt.shape[1])
    y_prompt, p_conv, p_delta, p_ret, p_c, p_n, p_m = run_group(
        x_prompt, pos_prompt, z_conv, z_delta, z_ret, z_c, z_n, z_m, p)
    pos_sample = PAST_LEN + jnp.arange(x_sample.shape[1])
    y_sample, s_conv, s_delta, s_ret, s_c, s_n, s_m = run_group(
        x_sample, pos_sample, state_conv_a, state_delta_a, state_ret_b, state_mlstm_C, state_mlstm_n, state_mlstm_m, p)
    return (y_prompt, y_sample, p_conv, p_delta, p_ret, p_c, p_n, p_m, s_conv, s_delta, s_ret, s_c, s_n, s_m)


_drawn_inputs = setup_inputs


def setup_inputs(seed=0):
    import zlib

    import numpy as np

    out = dict(_drawn_inputs(seed))
    spreads = {}
    factors = {'gdn_gain': 9.887,
     'ret_gain': 6.714,
     'mlstm_gain': 28.041,
     'final_gain': 7.836,
     'norm_ffn': 4.034}
    for name, (base, spread) in spreads.items():
        noise = np.random.default_rng([zlib.crc32(name.encode()), seed]).standard_normal(out[name].shape)
        drawn = base * np.exp(spread * noise) if base else spread * noise
        out[name] = __import__('jax').numpy.asarray(drawn.astype(out[name].dtype))
    for name, factor in factors.items():
        out[name] = (out[name] * factor).astype(out[name].dtype)
    return out
```

```python
from contextlib import ExitStack, contextmanager

import numpy as np
import concourse.bass as bass
from concourse import mybir

ALU = mybir.AluOpType
ACT = mybir.ActivationFunctionType
F32 = mybir.dt.float32
F32R = mybir.dt.float32r

P = 128
D_MODEL = 1024
SEQ = 1024
NB = 8
TOK = SEQ + NB
NT = 3
TT = TOK // NT
KC = D_MODEL // P
HEADS = 4
DK = 128
C = 128
NC_ = SEQ // C
LEVELS = 7
CONV_W = 4
D_FF = 4096
GROUPS = D_FF // D_MODEL
EPS = 1e-6
PAST_LEN = 8192
ROPE_BASE = 10000.0
QSCALE = DK ** -0.5

T_AB = 1
T_OUTA = T_AB + 2 * HEADS * 4
T_MLP0 = T_OUTA + KC
T_GC = T_MLP0 + GROUPS * 2 * KC
T_C = T_GC + 1
T_OUTC = T_C + HEADS * 6
T_MLP1 = T_OUTC + KC
TILES = T_MLP1 + GROUPS * 2 * KC

V_GAIN = {"mix_a": 0, "ffn0": 8, "mix_c": 16, "ffn1": 24, "final": 32}
V_GDN, V_RET, V_ML = 40, 41, 42
V_DTB, V_ALOG, V_BI, V_BF = 44, 45, 46, 47
V_CONV = 48
V_M0 = V_CONV + 48
V_N0 = V_M0 + NB
V_HIST = V_N0 + HEADS * NB
V_ALL = V_HIST + 12 * 3 * NB
K_ID, K_ONE, K_CAUS = 0, P, 2 * P
K_RG = 3 * P
K_RK = K_RG + 8
K_ALL = K_RK + 4


class Tally:

    def __init__(self, eng, step):
        self.eng, self.step = eng, step
        self.n, self.names, self.last = {}, {}, None
        self.i, self.per = None, {}

    def _value(self, key):
        value = self.n[key]
        if self.i is not None and self.per.get(key):
            value = self.i * self.per[key] + value
        return value

    def made(self, sem):
        key = sem.name
        self.n[key] = self.n.get(key, 0) + 1
        self.last = (sem, key)
        self.at = self._value(key)
        return sem, 1

    def stepped(self):
        return self.made(self.step)

    def settle(self):
        self.eng.wait_ge(self.last[0], self.at)

    def awaited(self, sem, by=1):
        key = "w " + sem.name
        self.n[key] = self.n.get(key, 0) + by
        return sem, self._value(key)

    @contextmanager
    def loop(self, count, per):
        start = dict(self.n)
        with self.eng.Fori(0, count) as i:
            self.i, self.per = i, per
            yield i
            self.i, self.per = None, {}
        for key, value in self.n.items():
            turn = value - start.get(key, 0)
            assert turn == per.get(key, 0), (key, turn, per.get(key, 0))
            self.n[key] = start.get(key, 0) + count * turn
        if self.last:
            self.at = self.n[self.last[1]]


def build(nc, io):
    with ExitStack() as ctx:
        def sem(name):
            return ctx.enter_context(nc.semaphore(name))

        base = (nc.sbuf_base + 31) // 32 * 32
        cursor = [base]

        def place(name, shape, dtype=F32, at=None):
            size = int(np.prod(shape[1:])) * 4
            if at is None:
                at = cursor[0]
                cursor[0] += (size + 31) // 32 * 32
            return nc.alloc_sbuf_tensor_at(name, list(shape), dtype, offset=at)

        R = TOK * 4
        raw = [place(f"w_raw{s}", [P, KC, P]) for s in range(2)]
        w_hi = [place(f"w_hi{s}", [P, KC, P], F32R) for s in range(2)]
        w_lo = [place(f"w_lo{s}", [P, KC, P], F32R) for s in range(2)]
        region = []
        ops = []
        for s in range(2):
            region.append(cursor[0])
            ops.append((place(f"x_hi{s}", [P, KC, TOK], F32R), place(f"x_lo{s}", [P, KC, TOK], F32R)))
        h_at = cursor[0]
        H = place("h", [P, KC, TOK])
        MIX = place("mix", [P, KC, TOK], at=h_at)
        extra = cursor[0]
        SSQ = place("ssq", [P, TOK])
        SQT = place("sq_third", [P, TOK])
        consts = place("consts", [P, K_ALL])
        vec = place("vec", [P, V_ALL])
        rbc = place("rbc", [P, TOK])
        gcol = place("gate_cols", [P, NC_, 36])
        negbe = place("neg_beta_eg", [P, NC_, HEADS])
        convo = place("conv_out_rows", [P, 12, 3 + 3 * NB])
        S = place("state", [P, 3 * P])
        resid = place("v_resid", [P, P])
        vnew = place("v_new", [P, P])
        small = place("small", [P, 12 * NB])
        kq = place("kq_sample", [P, NB, 2])
        krow = place("k_rows", [NB, P])
        vrow = place("v_rows", [NB, 2 * P])
        eps = place("eps", [P, 4])
        negea = place("neg_exp_a", [P, 1])
        assert cursor[0] <= nc.sbuf_usable_end, (cursor[0], nc.sbuf_usable_end)
        T_third = place("mlp_t", [P, TT], at=extra)
        U_third = place("mlp_u", [P, TT], at=extra + TT * 4)

        slots = []
        for layer in range(2):
            r0 = region[1 - layer]
            slots.append([place(f"s{layer}_{i}", [P, TOK], at=r0 + i * R) for i in range(16)]
                         + [place(f"s{layer}_{16 + i}", [P, TOK], at=extra + i * R) for i in range(2)])
        ss_c = place("sample_C", [P, NB, 2 * P], at=region[0] + 8 * R)
        levels = place("levels", [P, LEVELS, P], at=h_at + 6 * R)
        rows_a = place("gate_rows_a", [P, TOK], at=h_at + 7 * R)
        rows_c = place("gate_rows_c", [P, TOK], at=h_at + 7 * R)

        ident, ones, causal = (consts[:, k:k + P] for k in (K_ID, K_ONE, K_CAUS))

        PJ = ctx.enter_context(nc.psum_tensor("proj", [P, NT, 512], F32))
        MB = [ctx.enter_context(nc.psum_tensor(f"bank{b}", [P, 512], F32)) for b in range(5)]

        w_loaded = [sem("w_loaded0"), sem("w_loaded1")]
        w_hi_done, w_split = sem("w_hi_done"), sem("w_split")
        proj_full, proj_drained = sem("proj_full"), sem("proj_drained")
        x_ready = sem("x_ready")
        sq_made, ssq_added, rbc_ready = sem("sq_made"), sem("ssq_added"), sem("rbc_ready")
        consts_in, x_in, h_in = sem("consts_in"), sem("x_in"), [sem(f"h_in{i}") for i in range(KC)]
        h_spilled, mask_in, bconst_in = sem("h_spilled"), sem("mask_in"), sem("bconst_in")
        state_in, state_final, stored = sem("state_in"), sem("state_final"), sem("stored")
        dve_step, act_step = sem("dve_step"), sem("act_step")
        setup_done = sem("setup_done")
        to_act, to_dve, to_pe = sem("to_act"), sem("to_dve"), sem("to_pe")
        act_to_pe = sem("act_to_pe")
        y_done = sem("y_done")
        full = {r: [sem(f"full_{r}{b}") for b in range(5)] for r in ("dve", "act")}
        drained = {r: [sem(f"drained_{r}{b}") for b in range(5)] for r in ("dve", "act")}

        def third(a, tt):
            return a[:, tt * TT:(tt + 1) * TT]

        def chunk(a, c, n=1):
            return a[:, c * C:(c + n) * C]

        def rep(a, n):
            return a.unsqueeze(1).broadcast_to([a.shape[0], n, a.shape[1]])

        def spread(a, m):
            return a.unsqueeze(2).broadcast_to([a.shape[0], a.shape[1], m])

        def cut(a, n):
            return a.rearrange("p (n m) -> p n m", n=n)

        XR = {"mix0": 24, "xg1": 48, "hid0": 72, "xg2": 168, "mix1": 192, "xg3": 216, "hid1": 240}
        block = ctx.enter_context(nc.Block())

        @block.sync
        def _(sp):
            for t in range(2):
                sp.dma_start(raw[t][:], io["w_all"][t]).then_inc(w_loaded[t], 16)
            with sp.Fori(0, TILES // 2 - 1) as i:
                for s in range(2):
                    sp.wait_ge(w_split, 2 * i + s + 1)
                    sp.dma_start(raw[s][:], io["w_all"][2 * i + 2 + s]).then_inc(w_loaded[s], 16)

        @block.gpsimd
        def _(pool):
            def split(s, loads, done, free):
                pool.wait_ge(w_loaded[s], loads)
                if free is not None:
                    pool.wait_ge(proj_full, free)
                nc.gpsimd.tensor_tensor(w_hi[s][:], raw[s][:], rep(ones, KC), ALU.mult).then_inc(w_hi_done, 1)
                pool.wait_ge(w_hi_done, done)
                nc.gpsimd.tensor_tensor(w_lo[s][:], raw[s][:], w_hi[s][:].bitcast(F32),
                                        ALU.subtract).then_inc(w_split, 1)

            pool.wait_ge(consts_in, 32)
            for s in range(2):
                split(s, 16, s + 1, None)
            with pool.Fori(0, TILES // 2 - 1) as i:
                for s in range(2):
                    split(s, 16 * i + 32, 2 * i + s + 3, 6 * i + 3 * s + 3)

        @block.tensor
        def _(pe):
            n = Tally(pe, None)
            owner = [None] * 5

            def claim(b, reader):
                if owner[b]:
                    pe.wait_ge(drained[owner[b]][b], n.n["f" + owner[b] + str(b)])
                owner[b] = reader

            def publish(ins, b):
                key = "f" + owner[b] + str(b)
                n.n[key] = n.n.get(key, 0) + 1
                ins.then_inc(full[owner[b]][b], 1)

            def tile(t, slot, X, ready=None, first=False):
                hi, lo = X
                pe.wait_ge(w_split, t + 1)
                for tt in range(NT):
                    if not first:
                        pe.wait_ge(proj_drained, 3 * t + tt - 2)
                    for k in range(KC):
                        if ready is not None:
                            pe.wait_ge(x_ready, ready + 3 * k + tt + 1)
                        for j, (w, x) in enumerate(((w_hi, hi), (w_hi, lo), (w_lo, hi))):
                            last = nc.tensor.matmul(PJ[:, tt, 0:TT], w[slot][:, k, :],
                                                    x[:, k, tt * TT:(tt + 1) * TT],
                                                    start=(k == 0 and j == 0),
                                                    stop=(k == KC - 1 and j == 2))
                    last.then_inc(proj_full, 1)

            def norm_finish(number):
                pe.wait_ge(ssq_added, 21 * (number + 1))
                for tt in range(NT):
                    claim(tt, "act")
                    publish(nc.tensor.matmul(MB[tt][:, 0:TT], ones, third(SSQ, tt), start=True, stop=True), tt)

            def over_partitions(lhs, src, reader):
                for tt in range(NT):
                    claim(tt, reader)
                    publish(nc.tensor.matmul(MB[tt][:, 0:TT], lhs, third(src, tt), start=True, stop=True), tt)

            def per_chunk(b, reader, half, f):
                claim(b, reader)
                for q in range(4):
                    last = f(MB[b][:, q * C:(q + 1) * C], 4 * half + q)
                publish(last, b)

            def turned(b, reader, src, half):
                per_chunk(b, reader, half, lambda o, c: nc.tensor.transpose(o, chunk(src, c), ident))

            def mm(o, l, r, start=True, stop=True):
                return nc.tensor.matmul(o, l, r, start=start, stop=stop)

            def sel(row, rows):
                return consts[0:rows, K_ID + row:K_ID + row + 1].broadcast_to([rows, P])

            def sample_outer(values):
                pe.wait_ge(*n.awaited(to_pe))
                claim(4, "dve")
                nc.tensor.transpose(MB[4][0:NB, 0:P], small[:, 0:NB], ident)
                for j, v in enumerate(values):
                    last = nc.tensor.transpose(MB[4][0:NB, (j + 1) * P:(j + 2) * P], v, ident)
                publish(last, 4)

            def mixer_ab(s, h, delta):
                if delta:
                    over_partitions(sel(h, 36), rows_a[0:36, :], "dve")
                    over_partitions(sel(32 + h, 36), rows_a[0:36, :], "act")
                    for x in (10, 12):
                        pe.wait_ge(*n.awaited(act_to_pe))
                        over_partitions(ones, s[x], "act")
                q, k, v = (s[4], s[5], s[6]) if delta else (s[6], s[7], s[2])
                pe.wait_ge(*n.awaited(to_pe))
                for half in range(2):
                    turned(half, "dve", k, half)
                for half in range(2):
                    turned(2 + half, "dve", v, half)
                if delta:
                    for half in range(2):
                        per_chunk((4, 0)[half], "dve", half, lambda o, c: mm(o, chunk(k, c), chunk(s[14], c)))
                for half in range(2):
                    per_chunk(1 + half, "dve", half, lambda o, c: mm(o, chunk(k, c), chunk(q, c)))
                if delta:
                    LT, Pm, Dm, E = s[12], s[11], s[14], s[15]
                    for lv in range(LEVELS):
                        for half in range(2):
                            pe.wait_ge(*n.awaited(to_pe))
                            per_chunk(half, "dve", half,
                                      lambda o, c: mm(o, chunk(LT, c), chunk(Dm, c) if lv else ident))
                        for half in range(2):
                            pe.wait_ge(*n.awaited(to_pe))
                            if 0 < lv < LEVELS - 1:
                                per_chunk((2, 4)[half], "dve", half, lambda o, c: mm(o, chunk(E, c), chunk(Pm, c)))
                            per_chunk((3, half)[half], "dve", half,
                                      lambda o, c: mm(o, chunk(Pm, c), chunk(E, c) if lv else ident))
                Kd, V, qg, QKT = s[16], s[17], s[10], s[13]
                pe.wait_ge(*n.awaited(to_pe))
                for c in range(NC_):
                    if c:
                        pe.wait_ge(*n.awaited(to_pe))
                    if delta:
                        claim(0, "dve")
                        publish(mm(MB[0][:, 0:P], chunk(k, c), S[:, 0:P]), 0)
                    claim(2, "act")
                    mm(MB[2][:, 0:C], S[:, 0:P], chunk(qg, c), True, False)
                    if delta:
                        pe.wait_ge(*n.awaited(to_pe))
                        claim(1, "dve")
                        publish(mm(MB[1][:, 0:P], chunk(s[15], c), resid[:]), 1)
                        pe.wait_ge(*n.awaited(to_pe))
                    vv = vnew[:] if delta else chunk(V, c)
                    publish(mm(MB[2][:, 0:C], vv, chunk(QKT, c), False, True), 2)
                    claim(3, "dve")
                    publish(mm(MB[3][:, 0:P], chunk(Kd, c), vv), 3)
                pe.wait_ge(*n.awaited(to_pe))
                pe.wait_ge(state_in, n.awaited(state_in, 16)[1])
                claim(4, "dve")
                for b in range(NB):
                    mm(MB[4][:, 2 * b:2 * b + 2], s[9][:, b * P:(b + 1) * P], kq[:, b, :])
                publish(mm(MB[4][:, 2 * NB:3 * NB], ones, small[:, 0:NB]), 4)
                sample_outer([small[:, NB:2 * NB] if delta else v[:, SEQ:TOK]])
                pe.wait_ge(*n.awaited(to_pe))
                for half in range(2):
                    claim(half, "dve")
                    publish(mm(MB[half][:], krow[0:NB, :], s[13][0:NB, half * 512:(half + 1) * 512]), half)
                pe.wait_ge(*n.awaited(act_to_pe))
                over_partitions(ones, s[12], "act")

            def mixer_c(s, h):
                over_partitions(sel(h, 100), rows_c[0:100, :], "dve")
                claim(3, "dve")
                publish(mm(MB[3][:, 0:NB], sel(96 + h, 100), rows_c[0:100, SEQ:TOK]), 3)
                over_partitions(sel(32 + h, 100), rows_c[0:100, :], "act")
                over_partitions(sel(64 + h, 100), rows_c[0:100, :], "act")
                q, k = s[0], s[1]
                pe.wait_ge(*n.awaited(to_pe))
                for half in range(2):
                    turned(half, "dve", k, half)
                for half in range(2):
                    turned(2 + half, "dve", s[2], half)
                for half in range(2):
                    turned((4, 0)[half], "dve", s[3], half)
                for half in range(2):
                    per_chunk(1 + half, "dve", half, lambda o, c: mm(o, chunk(k, c), chunk(q, c)))
                Kd, V0, V1, qw, QKW = s[16], s[17], s[13], s[10], s[11]
                pe.wait_ge(*n.awaited(to_pe))
                for c in range(NC_):
                    if c:
                        pe.wait_ge(*n.awaited(to_pe))
                    for j, v in enumerate((chunk(V0, c), chunk(V1, c), ones)):
                        claim(j, "act")
                        mm(MB[j][:, 0:C], S[:, j * P:(j + 1) * P], chunk(qw, c), True, False)
                        publish(mm(MB[j][:, 0:C], v, chunk(QKW, c), False, True), j)
                    claim(3, "dve")
                    for j, v in enumerate((chunk(V0, c), chunk(V1, c), ones)):
                        last = mm(MB[3][:, j * P:(j + 1) * P], chunk(Kd, c), v)
                    publish(last, 3)
                pe.wait_ge(*n.awaited(to_pe))
                pe.wait_ge(state_in, n.awaited(state_in, 16)[1])
                claim(4, "dve")
                for b in range(NB):
                    for j in range(2):
                        mm(MB[4][:, j * NB + b:j * NB + b + 1], ss_c[:, b, j * P:(j + 1) * P], s[0][:, SEQ + b:SEQ + b + 1])
                mm(MB[4][:, 2 * NB:3 * NB], ones, small[:, 0:NB])
                publish(mm(MB[4][:, 3 * NB:4 * NB], ones, small[:, NB:2 * NB]), 4)
                sample_outer([s[2][:, SEQ:TOK], s[3][:, SEQ:TOK]])
                for j in range(2):
                    pe.wait_ge(*n.awaited(to_pe))
                    for half in range(2):
                        claim(half, "dve")
                        publish(mm(MB[half][:], krow[0:NB, :], s[11][0:NB, half * 512:(half + 1) * 512]), half)
                pe.wait_ge(*n.awaited(act_to_pe))
                for tt in range(NT):
                    claim(tt, "act")
                    mm(MB[tt][:, 0:TT], ones, third(s[10], tt), True, False)
                    publish(mm(MB[tt][:, 0:TT], ones, third(s[11], tt), False, True), tt)

            def mlp(t0, X, Y, ready, hid, number):
                with n.loop(GROUPS - 1, {}) as g:
                    for k in range(KC):
                        tile(t0 + 16 * g + k, (t0 + k) % 2, X, ready if k == 0 else None)
                        if k == 0:
                            pass
                    for k in range(KC):
                        tile(t0 + 16 * g + 8 + k, (t0 + k) % 2, Y, hid + 24 * g if k == 0 else None)
                g = GROUPS - 1
                for k in range(KC):
                    tile(t0 + 16 * g + k, (t0 + k) % 2, X)
                for k in range(KC):
                    tile(t0 + 16 * g + 8 + k, (t0 + k) % 2, Y, hid + 24 * g if k == 0 else None)
                norm_finish(number)

            def rows_turned(rows, count):
                pe.wait_ge(*n.awaited(to_pe))
                for half in range(2):
                    claim(half, "dve")
                    for q in range(4):
                        last = nc.tensor.transpose(MB[half][:, q * count:(q + 1) * count],
                                                   rows[0:count, (4 * half + q) * C:(4 * half + q + 1) * C],
                                                   consts[0:count, K_ID:K_ID + count])
                    publish(last, half)

            XA, XB = ops
            pe.wait_ge(setup_done, 1)
            pe.wait_ge(consts_in, 32)
            tile(0, 0, XA, 0, first=True)
            norm_finish(0)
            rows_turned(rows_a, 36)
            for u in range(2 * HEADS):
                for j in range(4):
                    t = T_AB + 4 * u + j
                    tile(t, t % 2, XA)
                mixer_ab(slots[0], u % HEADS, u < HEADS)
            for k in range(KC):
                tile(T_OUTA + k, (T_OUTA + k) % 2, XA, XR["mix0"] if k == 0 else None)
            norm_finish(1)
            mlp(T_MLP0, XB, XA, XR["xg1"], XR["hid0"], 2)
            tile(T_GC, T_GC % 2, XB, XR["xg2"])
            rows_turned(rows_c, 100)
            for u in range(HEADS):
                for j in range(6):
                    t = T_C + 6 * u + j
                    tile(t, t % 2, XB)
                mixer_c(slots[1], u)
            for k in range(KC):
                tile(T_OUTC + k, (T_OUTC + k) % 2, XB, XR["mix1"] if k == 0 else None)
            norm_finish(3)
            mlp(T_MLP1, XA, XB, XR["xg3"], XR["hid1"], 4)

        @block.vector
        def _(v):
            n = Tally(v, dve_step)
            tt_, ts_, stt = nc.vector.tensor_tensor, nc.vector.tensor_scalar, nc.vector.scalar_tensor_tensor

            def take(b):
                v.wait_ge(*n.awaited(full["dve"][b]))
                return MB[b]

            def done(b):
                return n.made(drained["dve"][b])

            def step(ins):
                ins.then_inc(*n.stepped())
                n.settle()

            def tell(sem):
                n.settle()
                v.sem_inc(*n.made(sem))

            def drain(t, tt, f):
                v.wait_ge(proj_full, 3 * t + tt + 1)
                f(PJ[:, tt, 0:TT], tt).then_inc(proj_drained, 1)

            def vcol(k):
                return vec[:, k:k + 1]

            def norm_chunk(c, tt, number, gain, X):
                hh = H[:, c, tt * TT:(tt + 1) * TT]
                if X is not None:
                    hi, lo = (x[:, c, tt * TT:(tt + 1) * TT] for x in X)
                    step(ts_(hi, hh, vcol(gain + c), None, ALU.mult))
                    stt(lo, hh, vcol(gain + c), hi.bitcast(F32), ALU.mult, ALU.subtract).then_inc(x_ready, 1)
                v.wait_ge(*n.awaited(sq_made))
                if c:
                    tt_(third(SSQ, tt), third(SSQ, tt), third(SQT, tt), ALU.add).then_inc(ssq_added, 1)
                    v.wait_ge(ssq_added, 21 * number + 3 * (c - 1) + tt + 1)

            def project(t, dst, scale=None):
                def f(ps, tt):
                    if scale is None:
                        return tt_(third(dst, tt), ps, third(rbc, tt), ALU.mult)
                    return stt(third(dst, tt), ps, scale, third(rbc, tt), ALU.mult, ALU.mult)
                for tt in range(NT):
                    drain(t, tt, f)

            def all_drained(t):
                v.wait_ge(proj_drained, 3 * t + 3)

            def residual(t0, c, number, gain, X, reload=False, wait=True):
                if reload:
                    v.wait_ge(h_in[c], 16 * reload)
                for tt in range(NT):
                    hh = H[:, c, tt * TT:(tt + 1) * TT]
                    drain(t0 + c, tt, lambda ps, tt: tt_(hh, hh, ps, ALU.add))
                    v.wait_ge(proj_drained, 3 * (t0 + c) + tt + 1)
                    norm_chunk(c, tt, number, gain, X)

            def mix_split(X, t_last):
                for c in range(KC):
                    for tt in range(NT):
                        hi, lo = (x[:, c, tt * TT:(tt + 1) * TT] for x in X)
                        m = MIX[:, c, tt * TT:(tt + 1) * TT]
                        step(nc.vector.tensor_copy(hi, m))
                        tt_(lo, m, hi.bitcast(F32), ALU.subtract).then_inc(x_ready, 1)

            def sample_outer(vm, j, pairs):
                step(tt_(cut(vm[0:NB, 0:NB * P], NB), rep(vrow[0:NB, j * P:(j + 1) * P], NB),
                         spread(consts[0:NB, K_ID:K_ID + NB], P), ALU.mult))

            def mixer_ab(s, h, delta, unit):
                v_in = s[2]
                if delta:
                    for x in range(3):
                        blk = x * HEADS + h
                        src, dst = s[x], s[4 + x]
                        w = V_CONV + 4 * blk
                        step(ts_(dst[:], src[:], vcol(w + 3), None, ALU.mult))
                        for i in range(3):
                            sh = 3 - i
                            step(stt(dst[:, sh:SEQ], src[:, 0:SEQ - sh], vcol(w + i), dst[:, sh:SEQ], ALU.mult, ALU.add))
                            hist = vec[:, V_HIST + (3 * blk + i) * NB:V_HIST + (3 * blk + i + 1) * NB]
                            step(stt(dst[:, SEQ:TOK], hist, vcol(w + i), dst[:, SEQ:TOK], ALU.mult, ALU.add))
                        nc.vector.tensor_copy(convo[:, blk, 0:3], src[:, SEQ - 3:SEQ])
                        nc.vector.tensor_copy(convo[:, blk, 3:3 + 2 * NB],
                                              vec[:, V_HIST + (3 * blk + 1) * NB:V_HIST + (3 * blk + 3) * NB])
                        nc.vector.tensor_copy(convo[:, blk, 3 + 2 * NB:], src[:, SEQ:TOK]).then_inc(*n.made(to_act))
                    for tt in range(NT):
                        ps = take(tt)
                        nc.vector.tensor_copy(third(s[7], tt), ps[:, 0:TT]).then_inc(*done(tt))
                    n.settle()
                    for c in range(NC_):
                        last = ts_(chunk(s[11], c), chunk(s[7], c), gcol[:, c, h:h + 1], 0.0, ALU.subtract, ALU.min)
                    last.then_inc(*n.made(to_act))
                    for x in range(3):
                        v.wait_ge(*n.awaited(to_dve))
                        stt(s[4 + x][:], (s[10], s[12], s[13])[x][:], 1.0, s[4 + x][:], ALU.add, ALU.mult).then_inc(*n.made(to_act))
                    v.wait_ge(*n.awaited(to_dve))
                    n.settle()
                    step(tt_(cut(s[11][:, 0:SEQ], NC_), cut(s[11][:, 0:SEQ], NC_), rep(causal, NC_), ALU.mult))
                    v.wait_ge(*n.awaited(to_dve))
                    step(stt(s[4][:], s[4][:], QSCALE, s[10][:], ALU.mult, ALU.mult))
                    step(tt_(s[10][:], s[4][:], s[7][:], ALU.mult))
                    v.wait_ge(*n.awaited(to_dve))
                    step(tt_(s[5][:], s[5][:], s[12][:], ALU.mult))
                    tt_(s[14][:], s[5][:], s[8][:], ALU.mult).then_inc(*n.made(to_pe))
                    q, k, v_in, OT = s[4], s[5], s[6], s[6]
                else:
                    if h == 0:
                        v.wait_ge(bconst_in, 48)
                    cos, sin = s[4], s[5]
                    for x in range(2):
                        rot = s[(12, 14)[x]]
                        v.wait_ge(*n.awaited(to_dve))
                        sc = 1.0 if x == 0 else QSCALE
                        step(stt(s[6 + x][:], s[x][:], sc, cos[:], ALU.mult, ALU.mult))
                        step(stt(rot[:], rot[:], sc, sin[:], ALU.mult, ALU.mult))
                        step(tt_(s[6 + x][:], s[6 + x][:], rot[:], ALU.add))
                    eg = s[8][:, 512 + h * P:512 + (h + 1) * P]
                    tt_(cut(s[10][:, 0:SEQ], NC_), cut(s[6][:, 0:SEQ], NC_), rep(eg, NC_), ALU.mult).then_inc(*n.made(to_pe))
                    q, k, OT = s[6], s[7], s[11]
                for half in range(2):
                    ps = take(half)
                    o = cut(chunk(s[16], 4 * half, 4), 4)
                    if delta:
                        tt_(o, cut(ps[:], 4), cut(chunk(s[11], 4 * half, 4), 4)[:, :, C - 1:C].broadcast_to([P, 4, C]),
                            ALU.mult).then_inc(*done(half))
                    else:
                        ts_(chunk(s[16], 4 * half, 4), ps[:], consts[:, K_RK + h:K_RK + h + 1], None, ALU.mult).then_inc(*done(half))
                for half in range(2):
                    ps = take(2 + half)
                    if delta:
                        tt_(cut(chunk(s[17], 4 * half, 4), 4), cut(ps[:], 4),
                            gcol[:, 4 * half:4 * half + 4, 32 + h:33 + h].broadcast_to([P, 4, C]), ALU.mult).then_inc(*done(2 + half))
                    else:
                        nc.vector.tensor_copy(chunk(s[17], 4 * half, 4), ps[:]).then_inc(*done(2 + half))
                if delta:
                    for half in range(2):
                        ps = take((4, 0)[half])
                        tt_(chunk(s[12], 4 * half, 4), ps[:], chunk(s[11], 4 * half, 4), ALU.mult).then_inc(*done((4, 0)[half]))
                for half in range(2):
                    ps = take(1 + half)
                    dec = cut(chunk(s[11], 4 * half, 4), 4) if delta else rep(s[8][:, h * P:(h + 1) * P], 4)
                    tt_(cut(chunk(s[13], 4 * half, 4), 4), cut(ps[:], 4), dec, ALU.mult).then_inc(*done(1 + half))
                if delta:
                    Pm, Dm, E = s[11], s[14], s[15]
                    n.settle()
                    for half in range(2):
                        tell(to_pe)
                    for lv in range(LEVELS):
                        for half in range(2):
                            ps = take(half)
                            tt_(cut(chunk(Pm, 4 * half, 4), 4), cut(ps[:], 4), rep(levels[:, lv, :], 4), ALU.mult).then_inc(*done(half))
                            n.settle()
                            if lv == 0:
                                tt_(cut(chunk(Dm, 4 * half, 4), 4), rep(ident, 4), cut(chunk(Pm, 4 * half, 4), 4), ALU.subtract).then_inc(*n.made(to_pe))
                            else:
                                tell(to_pe)
                        for half in range(2):
                            if 0 < lv < LEVELS - 1:
                                b = (2, 4)[half]
                                ps = take(b)
                                d = chunk(Dm, 4 * half, 4)
                                tt_(d, d, ps[:], ALU.subtract).then_inc(*done(b))
                            b = (3, half)[half]
                            ps = take(b)
                            e = cut(chunk(E, 4 * half, 4), 4)
                            tt_(e, e if lv else rep(ident, 4), cut(ps[:], 4), ALU.subtract).then_inc(*done(b))
                            n.settle()
                            if lv < LEVELS - 1:
                                tell(to_pe)
                n.settle()
                nc.vector.memset(S[:, 0:P], 0.0).then_inc(*n.made(to_pe))
                for c in range(NC_):
                    if delta:
                        ps = take(0)
                        stt(resid[:], ps[:, 0:P], negbe[:, c, h:h + 1], chunk(s[17], c), ALU.mult, ALU.add).then_inc(*done(0))
                        n.settle()
                        tell(to_pe)
                        ps = take(1)
                        nc.vector.tensor_copy(vnew[:], ps[:, 0:P]).then_inc(*done(1))
                        n.settle()
                        tell(to_pe)
                    ps = take(3)
                    gl = s[7][:, c * C + C - 1:c * C + C] if delta else consts[:, K_RG + 4 + h:K_RG + 5 + h]
                    stt(S[:, 0:P], S[:, 0:P], gl, ps[:, 0:P], ALU.mult, ALU.add).then_inc(*done(3))
                    n.settle()
                    if c < NC_ - 1:
                        tell(to_pe)
                qs, ks, vs = q[:, SEQ:TOK], k[:, SEQ:TOK], v_in[:, SEQ:TOK]
                sm = [small[:, j * NB:(j + 1) * NB] for j in range(12)]
                nc.vector.tensor_copy(kq[:, :, 0], ks)
                nc.vector.tensor_copy(kq[:, :, 1], qs)
                tt_(sm[0], qs, ks, ALU.mult).then_inc(*n.made(to_pe))
                ps = take(4)
                step(nc.vector.tensor_copy(small[:, 4 * NB:7 * NB], ps[:, 0:3 * NB]))
                nc.vector.tensor_copy(sm[0], ks).then_inc(*done(4))
                KS = small[:, 4 * NB:6 * NB].rearrange("p (b two) -> p b two", two=2)[:, :, 0]
                QS = small[:, 4 * NB:6 * NB].rearrange("p (b two) -> p b two", two=2)[:, :, 1]
                if delta:
                    egs, bbs = s[7][:, SEQ:TOK], s[8][:, SEQ:TOK]
                    step(tt_(sm[2], KS, egs, ALU.mult))
                    step(tt_(sm[2], vs, sm[2], ALU.subtract))
                    step(tt_(sm[1], sm[2], bbs, ALU.mult))
                    vs = sm[1]
                    step(tt_(sm[2], QS, egs, ALU.mult))
                else:
                    step(ts_(sm[2], QS, consts[:, K_RG + h:K_RG + h + 1], None, ALU.mult))
                step(tt_(sm[3], sm[6], vs, ALU.mult))
                tt_(OT[:, SEQ:TOK] if not delta else sm[7], sm[2], sm[3], ALU.add).then_inc(*n.made(to_pe))
                ps = take(4)
                step(nc.vector.tensor_copy(krow[:], ps[0:NB, 0:P]))
                nc.vector.tensor_copy(vrow[:, 0:P], ps[0:NB, P:2 * P]).then_inc(*done(4))
                n.settle()
                if delta:
                    step(nc.vector.tensor_copy(OT[:, SEQ:TOK], sm[7]))
                sample_outer(s[13], 0, 1)
                tell(to_pe)
                SS = cut(s[9][:, 0:NB * P], NB)
                v.wait_ge(state_in, n.awaited(state_in, 16)[1])
                if delta:
                    step(tt_(SS, SS, spread(egs, P), ALU.mult))
                else:
                    step(ts_(s[9][:, 0:NB * P], s[9][:, 0:NB * P], consts[:, K_RG + h:K_RG + h + 1], None, ALU.mult))
                for half in range(2):
                    ps = take(half)
                    x = s[9][:, half * 512:(half + 1) * 512]
                    tt_(x, x, ps[:], ALU.add).then_inc(*done(half))
                n.settle()
                tell(to_act)
                v.wait_ge(*n.awaited(to_dve))
                step(tt_(OT[:], OT[:], s[12][:], ALU.mult))
                step(stt(s[3][:], s[13][:], 1.0, s[3][:], ALU.add, ALU.mult))
                step(stt(MIX[:, unit, :], OT[:], vcol(V_GDN if delta else V_RET), s[3][:], ALU.mult, ALU.mult))
                v.wait_ge(stored, n.awaited(stored, 32)[1])

            def mixer_c(s, h):
                q, k = s[0], s[1]
                for tt in range(NT):
                    ps = take(tt)
                    nc.vector.tensor_copy(third(s[12], tt), ps[:, 0:TT]).then_inc(*done(tt))
                n.settle()
                for c in range(NC_):
                    last = ts_(chunk(s[11], c), chunk(s[12], c), gcol[:, c, h:h + 1], 0.0, ALU.add, ALU.min)
                ps = take(3)
                tt_(small[:, 8 * NB:9 * NB], ps[:, 0:NB], s[12][:, SEQ:TOK], ALU.add).then_inc(*done(3))
                n.settle()
                tell(to_act)
                v.wait_ge(*n.awaited(to_dve))
                step(tt_(cut(s[11][:, 0:SEQ], NC_), cut(s[11][:, 0:SEQ], NC_), rep(causal, NC_), ALU.mult))
                tt_(s[10][:], q[:], s[6][:], ALU.mult).then_inc(*n.made(to_pe))
                for half in range(2):
                    ps = take(half)
                    tt_(cut(chunk(s[16], 4 * half, 4), 4), cut(ps[:], 4),
                        cut(chunk(s[11], 4 * half, 4), 4)[:, :, C - 1:C].broadcast_to([P, 4, C]), ALU.mult).then_inc(*done(half))
                for half in range(2):
                    ps = take(2 + half)
                    nc.vector.tensor_copy(chunk(s[17], 4 * half, 4), ps[:]).then_inc(*done(2 + half))
                for half in range(2):
                    b = (4, 0)[half]
                    ps = take(b)
                    nc.vector.tensor_copy(chunk(s[13], 4 * half, 4), ps[:]).then_inc(*done(b))
                n.settle()
                for half in range(2):
                    ps = take(1 + half)
                    x = chunk(s[11], 4 * half, 4)
                    tt_(x, ps[:], x, ALU.mult).then_inc(*done(1 + half))
                n.settle()
                nc.vector.memset(S[:], 0.0).then_inc(*n.made(to_pe))
                for c in range(NC_):
                    ps = take(3)
                    stt(S[:], S[:], s[6][:, c * C + C - 1:c * C + C], ps[:, 0:3 * P], ALU.mult, ALU.add).then_inc(*done(3))
                    n.settle()
                    if c < NC_ - 1:
                        tell(to_pe)
                qs, ks = q[:, SEQ:TOK], k[:, SEQ:TOK]
                sm = [small[:, j * NB:(j + 1) * NB] for j in range(12)]
                n0 = vec[:, V_N0 + h * NB:V_N0 + (h + 1) * NB]
                step(tt_(sm[1], n0, qs, ALU.mult))
                tt_(sm[0], qs, ks, ALU.mult).then_inc(*n.made(to_pe))
                ps = take(4)
                step(nc.vector.tensor_copy(small[:, 4 * NB:8 * NB], ps[:, 0:4 * NB]))
                tt_(sm[0], ks, sm[8], ALU.mult).then_inc(*done(4))
                n.settle()
                tell(to_pe)
                ws = s[6][:, SEQ:TOK]
                step(tt_(sm[2], sm[6], sm[8], ALU.mult))
                for j in range(2):
                    step(tt_(sm[4 + j], sm[4 + j], ws, ALU.mult))
                    step(tt_(sm[9], sm[2], s[2 + j][:, SEQ:TOK], ALU.mult))
                    step(tt_(s[(12, 14)[j]][:, SEQ:TOK], sm[4 + j], sm[9], ALU.add))
                step(tt_(sm[7], sm[7], ws, ALU.mult))
                step(tt_(sm[7], sm[7], sm[2], ALU.add))
                step(stt(s[15][:, SEQ:TOK], sm[7], -1.0, sm[7], ALU.mult, ALU.max))
                step(tt_(n0, n0, ws, ALU.mult))
                step(tt_(n0, n0, sm[0], ALU.add))
                ps = take(4)
                step(nc.vector.tensor_copy(krow[:], ps[0:NB, 0:P]))
                nc.vector.tensor_copy(vrow[:], ps[0:NB, P:3 * P]).then_inc(*done(4))
                n.settle()
                v.wait_ge(state_in, n.awaited(state_in, 16)[1])
                step(tt_(ss_c[:], ss_c[:], spread(ws, 2 * P), ALU.mult))
                for j in range(2):
                    sample_outer(s[11], j, 1)
                    tell(to_pe)
                    for half in range(2):
                        ps = take(half)
                        x = ss_c[:, 4 * half:4 * half + 4, j * P:(j + 1) * P]
                        tt_(x, x, cut(ps[:], 4), ALU.add).then_inc(*done(half))
                n.settle()
                tell(to_act)
                v.wait_ge(*n.awaited(to_dve))
                step(tt_(s[15][:], s[15][:], s[7][:], ALU.max))
                step(nc.vector.reciprocal(s[15][:], s[15][:]))
                step(tt_(s[12][:], s[12][:], s[15][:], ALU.mult))
                tt_(s[14][:], s[14][:], s[15][:], ALU.mult).then_inc(*n.made(to_act))
                v.wait_ge(*n.awaited(to_dve))
                for j in range(2):
                    x = s[(12, 14)[j]]
                    step(stt(x[:], x[:], vcol(V_ML + j), s[10][:], ALU.mult, ALU.mult))
                    step(stt(MIX[:, 2 * h + j, :], s[16 + j][:], 1.0, x[:], ALU.add, ALU.mult))
                v.wait_ge(stored, n.awaited(stored, 64)[1])

            def mlp(t0, X, Y, number, gain, Xn):
                def up(t, c):
                    for tt in range(NT):
                        drain(t, tt, lambda ps, tt: tt_(T_third[:], ps, third(rbc, tt), ALU.mult))
                        v.wait_ge(proj_drained, 3 * t + tt + 1)
                        step(stt(U_third[:], T_third[:], 0.0, T_third[:], ALU.max, ALU.mult))
                        hi, lo = (y[:, c, tt * TT:(tt + 1) * TT] for y in Y)
                        step(nc.vector.tensor_copy(hi, U_third[:]))
                        tt_(lo, U_third[:], hi.bitcast(F32), ALU.subtract).then_inc(x_ready, 1)

                v.wait_ge(*n.awaited(rbc_ready))
                with n.loop(GROUPS - 1, {dve_step.name: 2 * NT * KC}) as g:
                    for c in range(KC):
                        up(t0 + 16 * g + c, c)
                    for c in range(KC):
                        for tt in range(NT):
                            hh = H[:, c, tt * TT:(tt + 1) * TT]
                            drain(t0 + 16 * g + 8 + c, tt, lambda ps, tt: tt_(hh, hh, ps, ALU.add))
                t1 = t0 + 16 * (GROUPS - 1)
                for c in range(KC):
                    up(t1 + c, c)
                v.wait_ge(x_ready, XR["hid0" if number == 2 else "hid1"] + 24 * GROUPS)
                for c in range(KC):
                    residual(t1 + 8, c, number, gain, Xn)

            XA, XB = ops
            nc.vector.memset(eps[:, 0:1], EPS)
            nc.vector.memset(eps[:, 1:2], 1.0)
            v.wait_ge(consts_in, 32)
            for a, m in ((V_CONV, 48), (V_GDN, 4)):
                last = ts_(vec[:, a:a + m], vec[:, a:a + m], 0.5, None, ALU.mult)
            last.then_inc(setup_done, 1)
            v.wait_ge(x_in, 16 * KC)
            for c in range(KC):
                for tt in range(NT):
                    norm_chunk(c, tt, 0, V_GAIN["mix_a"], XA)
            s = slots[0]
            step(nc.vector.memset(rows_a[0:36, :], 0.0))
            v.wait_ge(*n.awaited(rbc_ready))
            for tt in range(NT):
                v.wait_ge(proj_full, tt + 1)
                step(tt_(s[12][0:HEADS, tt * TT:(tt + 1) * TT], PJ[0:HEADS, tt, 0:TT], rbc[0:HEADS, tt * TT:(tt + 1) * TT], ALU.mult))
                tt_(rows_a[32:36, tt * TT:(tt + 1) * TT], PJ[32:36, tt, 0:TT],
                    rbc[32:36, tt * TT:(tt + 1) * TT], ALU.mult).then_inc(proj_drained, 1)
            v.wait_ge(proj_drained, NT)
            a = s[12][0:HEADS, :]
            ts_(a, a, vec[0:HEADS, V_DTB:V_DTB + 1], None, ALU.add).then_inc(*n.made(to_act))
            n.settle()
            v.wait_ge(*n.awaited(to_dve))
            step(ts_(negea[0:HEADS, :], negea[0:HEADS, :], -1.0, None, ALU.mult))
            step(stt(a, a, 0.0, s[13][0:HEADS, :], ALU.max, ALU.add))
            step(ts_(a, a, negea[0:HEADS, :], None, ALU.mult))
            v.wait_ge(mask_in, 16)
            step(nc.vector.tensor_tensor_scan(rows_a[0:HEADS, :], s[11][0:HEADS, :], a, 0.0, ALU.mult, ALU.add))
            ts_(rows_a[32:36, :], rows_a[32:36, :], 0.5, 0.5, ALU.mult, ALU.add).then_inc(*n.made(to_pe))
            for half in range(2):
                ps = take(half)
                nc.vector.tensor_copy(gcol[:, 4 * half:4 * half + 4, :], cut(ps[:, 0:4 * 36], 4)).then_inc(*done(half))
            n.settle()
            tell(to_act)
            v.wait_ge(*n.awaited(to_dve))
            step(stt(negbe[:], negbe[:], -1.0, gcol[:, :, 32:36], ALU.mult, ALU.mult))
            v.wait_ge(mask_in, 32)
            for u in range(2 * HEADS):
                for j in range(4):
                    project(T_AB + 4 * u + j, s[j])
                all_drained(T_AB + 4 * u + 3)
                tell(to_act)
                mixer_ab(s, u % HEADS, u < HEADS, u)
            mix_split(XA, T_OUTA - 1)
            for c in range(KC):
                residual(T_OUTA, c, 1, V_GAIN["ffn0"], XB, reload=1)
            mlp(T_MLP0, XB, XA, 2, V_GAIN["mix_c"], XB)
            s = slots[1]
            v.wait_ge(*n.awaited(rbc_ready))
            v.wait_ge(h_spilled, 16 * KC)
            step(nc.vector.memset(rows_c[0:100, :], 0.0))
            I, F, B, Mr = (s[j][0:HEADS, :] for j in (12, 13, 14, 15))
            for tt in range(NT):
                v.wait_ge(proj_full, 3 * T_GC + tt + 1)
                step(tt_(I[:, tt * TT:(tt + 1) * TT], PJ[0:HEADS, tt, 0:TT], rbc[0:HEADS, tt * TT:(tt + 1) * TT], ALU.mult))
                tt_(F[:, tt * TT:(tt + 1) * TT], PJ[32:36, tt, 0:TT], rbc[32:36, tt * TT:(tt + 1) * TT],
                    ALU.mult).then_inc(proj_drained, 1)
            all_drained(T_GC)
            step(ts_(I, I, vec[0:HEADS, V_BI:V_BI + 1], None, ALU.add))
            ts_(F, F, vec[0:HEADS, V_BF:V_BF + 1], None, ALU.add).then_inc(*n.made(to_act))
            n.settle()
            v.wait_ge(*n.awaited(to_dve))
            step(stt(F, F, 0.0, s[16][0:HEADS, :], ALU.min, ALU.subtract))
            v.wait_ge(mask_in, 48)
            step(nc.vector.tensor_tensor_scan(B, s[11][0:HEADS, :], F, 0.0, ALU.mult, ALU.add))
            step(nc.vector.tensor_tensor_scan(Mr[:, 0:SEQ], F[:, 0:SEQ], I[:, 0:SEQ], 0.0, ALU.add, ALU.max))
            m0 = vec[0:HEADS, V_M0:V_M0 + NB]
            step(tt_(Mr[:, SEQ:TOK], F[:, SEQ:TOK], m0, ALU.add))
            step(tt_(Mr[:, SEQ:TOK], Mr[:, SEQ:TOK], I[:, SEQ:TOK], ALU.max))
            step(tt_(rows_c[0:HEADS, :], B, Mr, ALU.subtract))
            r1 = rows_c[0:HEADS, :]
            nc.vector.tensor_copy(rows_c[32:36, 0:C], r1[:, 0:C])
            tt_(cut(rows_c[32:36, C:SEQ], NC_ - 1), cut(r1[:, C:SEQ], NC_ - 1),
                cut(Mr[:, 0:SEQ - C], NC_ - 1)[:, :, C - 1:C].broadcast_to([HEADS, NC_ - 1, C]), ALU.add)
            tt_(rows_c[32:36, SEQ:TOK], r1[:, SEQ:TOK], m0, ALU.add)
            ts_(rows_c[64:68, :], Mr, -1.0, None, ALU.mult)
            tt_(rows_c[96:100, :], I, B, ALU.subtract).then_inc(*n.made(to_pe))
            n.settle()
            tell(to_act)
            for half in range(2):
                ps = take(half)
                nc.vector.tensor_copy(gcol[:, 4 * half:4 * half + 4, 0:HEADS],
                                      cut(ps[:, 0:400], 4)[:, :, 96:100]).then_inc(*done(half))
            n.settle()
            v.wait_ge(stored, n.awaited(stored, 48)[1])
            for u in range(HEADS):
                for j in range(6):
                    project(T_C + 6 * u + j, s[j], QSCALE if j == 1 else None)
                all_drained(T_C + 6 * u + 5)
                tell(to_act)
                mixer_c(s, u)
            mix_split(XB, T_OUTC - 1)
            for c in range(KC):
                residual(T_OUTC, c, 3, V_GAIN["ffn1"], XA, reload=2)
            mlp(T_MLP1, XA, XB, 4, V_GAIN["final"], None)
            v.wait_ge(*n.awaited(rbc_ready))
            for c in range(KC):
                stt(H[:, c, :], H[:, c, :], vcol(V_GAIN["final"] + c), rbc[:], ALU.mult, ALU.mult).then_inc(y_done, 1)

        @block.scalar
        def _(a):
            n = Tally(a, act_step)
            act = nc.scalar.activation
            LNEXP = "natural_log_exp_and_others"

            def take(b):
                a.wait_ge(*n.awaited(full["act"][b]))
                return MB[b]

            def done(b):
                return n.made(drained["act"][b])

            def step(ins):
                ins.then_inc(*n.stepped())
                n.settle()

            def tell(sem):
                n.settle()
                a.sem_inc(*n.made(sem))

            def rsqrt_of_banks(dst, scale, sig):
                for tt in range(NT):
                    ps = take(tt)
                    act(third(dst, tt), ps[:, 0:TT], ACT.Ln, bias=eps[:, 0:1], scale=scale).then_inc(*done(tt))
                n.settle()
                act(dst[:], dst[:], ACT.Exp, scale=-0.5).then_inc(*n.made(sig))

            def squares(c, tt, number):
                hh = H[:, c, tt * TT:(tt + 1) * TT]
                if c >= 2:
                    a.wait_ge(ssq_added, 21 * number + 3 * (c - 2) + tt + 1)
                act(third(SQT if c else SSQ, tt), hh, ACT.Square).then_inc(sq_made, 1)

            def norm_of(t0, number, after=None):
                for c in range(KC):
                    for tt in range(NT):
                        a.wait_ge(proj_drained, 3 * (t0 + c) + tt + 1)
                        squares(c, tt, number)
                    if after:
                        after(c)
                rsqrt_of_banks(rbc, 1.0 / D_MODEL, rbc_ready)

            def store(dst, src):
                a.dma_start(dst, src).then_inc(stored, 16)

            def mixer_ab(s, h, delta):
                a.wait_ge(*n.awaited(to_act))
                a.dma_start(s[9][:, 0:NB * P], io["state_a" if delta else "state_b"][h]).then_inc(state_in, 16)
                if delta:
                    a.wait_ge(to_act, n.awaited(to_act, 3)[1])
                    a.wait_ge(*n.awaited(to_act))
                    for x in range(3):
                        act((s[10], s[12], s[13])[x][:], s[4 + x][:], ACT.Tanh, scale=0.5 * 2).then_inc(*n.made(to_dve))
                    act(s[7][:], s[7][:], ACT.Exp)
                    act(s[11][:, 0:SEQ], s[11][:, 0:SEQ], ACT.Exp)
                    for tt in range(NT):
                        ps = take(tt)
                        act(third(s[8], tt), ps[:, 0:TT], ACT.Copy).then_inc(*done(tt))
                    n.settle()
                    tell(to_dve)
                    a.wait_ge(to_act, n.awaited(to_act, 3)[1])
                    for x, sq in ((4, 10), (5, 12)):
                        act(s[sq][:], s[x][:], ACT.Square).then_inc(*n.made(act_to_pe))
                    nc.scalar.preload_act_table_set(LNEXP)
                    for sq in (10, 12):
                        rsqrt_of_banks(s[sq], 1.0, to_dve)
                    OT = s[6]
                else:
                    for x in range(2):
                        rot = s[(12, 14)[x]]
                        act(rot[0:64, :], s[x][64:128, :], ACT.Copy)
                        act(rot[64:128, :], s[x][0:64, :], ACT.Copy).then_inc(*n.made(to_dve))
                    OT = s[11]
                for c in range(NC_):
                    ps = take(2)
                    act(chunk(OT, c), ps[:, 0:C], ACT.Copy).then_inc(*done(2))
                n.settle()
                a.wait_ge(*n.awaited(to_act))
                store(io["s_state_a" if delta else "s_state_b"][h], s[9][:, 0:NB * P])
                store(io["p_state_a" if delta else "p_state_b"][h], S[:, 0:P])
                act(s[12][:], OT[:], ACT.Square).then_inc(*n.made(act_to_pe))
                act(s[13][:], s[3][:], ACT.Tanh, scale=0.5)
                nc.scalar.preload_act_table_set(LNEXP)
                rsqrt_of_banks(s[12], 1.0 / DK, to_dve)

            def mixer_c(s, h):
                a.wait_ge(*n.awaited(to_act))
                a.dma_start(ss_c[:], io["state_c"][h].rearrange("p (b v) -> p b v", b=NB)).then_inc(state_in, 16)
                a.wait_ge(*n.awaited(to_act))
                act(s[11][:, 0:SEQ], s[11][:, 0:SEQ], ACT.Exp)
                act(small[:, 8 * NB:9 * NB], small[:, 8 * NB:9 * NB], ACT.Exp)
                for dst in (s[6], s[7]):
                    for tt in range(NT):
                        ps = take(tt)
                        act(third(dst, tt), ps[:, 0:TT], ACT.Exp).then_inc(*done(tt))
                n.settle()
                tell(to_dve)
                for c in range(NC_):
                    for j, (x, f) in enumerate(((12, ACT.Copy), (14, ACT.Copy), (15, ACT.Abs))):
                        ps = take(j)
                        act(chunk(s[x], c), ps[:, 0:C], f).then_inc(*done(j))
                n.settle()
                a.wait_ge(*n.awaited(to_act))
                tell(to_dve)
                store(io["s_state_c"][h].rearrange("p (b v) -> p b v", b=NB), ss_c[:])
                store(io["p_state_c"][h], S[:, 0:2 * P])
                store(io["p_n"][h], S[:, 2 * P:2 * P + 1])
                store(io["s_n"][h], vec[:, V_N0 + h * NB:V_N0 + (h + 1) * NB])
                a.wait_ge(*n.awaited(to_act))
                act(s[10][:], s[12][:], ACT.Square)
                act(s[11][:], s[14][:], ACT.Square).then_inc(*n.made(act_to_pe))
                for j in range(2):
                    act(s[16 + j][:], s[4 + j][:], ACT.Tanh, scale=0.5)
                nc.scalar.preload_act_table_set(LNEXP)
                rsqrt_of_banks(s[10], 1.0 / (2 * P), to_dve)

            a.dma_start(consts[:], io["consts"]).then_inc(consts_in, 16)
            a.dma_start(vec[:], io["vec"]).then_inc(consts_in, 16)
            for c in range(KC):
                a.dma_start(H[:, c, :], io["x"][c]).then_inc(x_in, 16)
            a.dma_start(slots[0][11][0:HEADS, :], io["scan_mask"]).then_inc(mask_in, 16)
            a.wait_ge(setup_done, 1)
            a.wait_ge(x_in, 16 * KC)
            for c in range(KC):
                for tt in range(NT):
                    squares(c, tt, 0)
            nc.scalar.preload_act_table_set(LNEXP)
            rsqrt_of_banks(rbc, 1.0 / D_MODEL, rbc_ready)
            a.wait_ge(x_ready, 24)
            a.wait_ge(mask_in, 16)
            a.dma_start(levels[:], io["levels"].rearrange("p (l m) -> p l m", l=LEVELS)).then_inc(mask_in, 16)
            s = slots[0]
            a.wait_ge(*n.awaited(to_act))
            t = s[13][0:HEADS, :]
            step(act(t, s[12][0:HEADS, :], ACT.Abs))
            step(act(t, t, ACT.Exp, scale=-1.0))
            act(negea[0:HEADS, :], vec[0:HEADS, V_ALOG:V_ALOG + 1], ACT.Exp)
            step(act(t, t, ACT.Ln, bias=eps[0:HEADS, 1:2]))
            act(rows_a[32:36, :], rows_a[32:36, :], ACT.Tanh, scale=0.5).then_inc(*n.made(to_dve))
            a.wait_ge(*n.awaited(to_act))
            act(negbe[:], gcol[:, :, 0:HEADS], ACT.Exp).then_inc(*n.made(to_dve))
            for u in range(2 * HEADS):
                if u == HEADS:
                    a.wait_ge(proj_drained, 3 * (T_AB + 4 * u))
                    a.dma_start(s[4][:], io["cos"]).then_inc(bconst_in, 16)
                    a.dma_start(s[5][:], io["sin"]).then_inc(bconst_in, 16)
                    a.dma_start(s[8][:, 0:8 * P], io["retention"]).then_inc(bconst_in, 16)
                mixer_ab(s, u % HEADS, u < HEADS)
            def reload(src, base):
                for c in range(KC):
                    a.wait_ge(x_ready, base + 3 * c + 3)
                    a.dma_start(H[:, c, :], src[c]).then_inc(h_in[c], 16)

            reload(io["x"], XR["mix0"])
            store(io["conv_rows"], convo[:].rearrange("p a b -> p (a b)"))
            norm_of(T_OUTA, 1)

            def spill(c):
                a.dma_start(io["h_spill"][c], H[:, c, :]).then_inc(h_spilled, 16)

            norm_of(T_MLP0 + 16 * (GROUPS - 1) + 8, 2, spill)
            s = slots[1]
            a.dma_start(s[11][0:HEADS, :], io["scan_mask"]).then_inc(mask_in, 16)
            a.wait_ge(*n.awaited(to_act))
            t = s[16][0:HEADS, :]
            step(act(t, s[13][0:HEADS, :], ACT.Abs))
            step(act(t, t, ACT.Exp, scale=-1.0))
            act(t, t, ACT.Ln, bias=eps[0:HEADS, 1:2]).then_inc(*n.made(to_dve))
            a.wait_ge(*n.awaited(to_act))
            store(io["p_m"], s[15][0:HEADS, SEQ - 1:SEQ])
            store(io["s_m"], s[15][0:HEADS, SEQ:TOK])
            for u in range(HEADS):
                mixer_c(s, u)
            reload(io["h_spill"], XR["mix1"])
            norm_of(T_OUTC, 3)
            norm_of(T_MLP1 + 16 * (GROUPS - 1) + 8, 4)
            for c in range(KC):
                a.wait_ge(y_done, c + 1)
                a.dma_start(io["y"][c], H[:, c, :]).then_inc(stored, 16)
            total = 16 * (2 * 2 * HEADS + 1 + 2 + 4 * HEADS + KC)
            a.wait_ge(stored, total)
            a.wait_ge(h_spilled, 16 * KC)


def shape_constants():
    f = np.float32
    i = np.arange(P)
    consts = np.zeros((P, K_ALL), f)
    consts[:, K_ID:K_ID + P] = np.eye(P)
    consts[:, K_ONE:K_ONE + P] = 1
    consts[:, K_CAUS:K_CAUS + P] = i[:, None] <= i[None, :]
    lg = np.log1p(-np.exp2(-5.0 - np.arange(HEADS, dtype=np.float64)))
    consts[:, K_RG:K_RG + 4] = np.exp(lg)
    consts[:, K_RG + 4:K_RG + 8] = np.exp(C * lg)
    consts[:, K_RK:K_RK + 4] = np.exp(lg[None, :] * (C - 1 - i)[:, None])
    levels = np.zeros((P, LEVELS, P), f)
    for lv in range(LEVELS):
        b = 1 << lv
        levels[:, lv, :] = ((i[:, None] // (2 * b) == i[None, :] // (2 * b))
                            & (i[:, None] // b % 2 == 1) & (i[None, :] // b % 2 == 0))
    ret = np.zeros((P, 2, HEADS, P), f)
    diff = (i[None, :] - i[:, None])
    for h in range(HEADS):
        ret[:, 0, h] = np.where(diff >= 0, np.exp(lg[h] * np.maximum(diff, 0)), 0)
        ret[:, 1, h] = np.exp(lg[h] * (i + 1))[None, :]
    half = DK // 2
    inv = (f(ROPE_BASE) ** (-np.arange(half, dtype=f) / f(half))).astype(f)
    pos = np.concatenate([np.arange(SEQ), np.full(NB, PAST_LEN)]).astype(f)
    ang = (inv[:, None] * pos[None, :]).astype(f).astype(np.float64)
    cos = np.concatenate([np.cos(ang)] * 2).astype(f)
    sin = np.concatenate([-np.sin(ang), np.sin(ang)]).astype(f)
    mask = np.ones((HEADS, TOK), f)
    mask[:, 0:SEQ:C] = 0
    mask[:, SEQ:] = 0
    return {"consts": consts, "levels": levels.reshape(P, -1), "retention": ret.reshape(P, -1),
            "cos": cos, "sin": sin, "scan_mask": mask}


def kernel(x_prompt, x_sample, state_conv_a, state_delta_a, state_ret_b, state_mlstm_C, state_mlstm_n, state_mlstm_m,
           norm_mix_a, w_in_a, w_conv_a, a_log, dt_bias, gdn_gain, ret_gain, w_out_a,
           norm_mix_c, w_in_c, b_gate_c, mlstm_gain, w_out_c, norm_ffn, w_up, w_down, final_gain):
    import concourse.bacc as bacc
    from concourse.bass_utils import run_bass_kernel_spmd

    def arr(a):
        return np.asarray(a)

    f = np.float32

    def tiles_of(w, rows, cols):
        w = arr(w)[rows:rows + D_MODEL]
        return [w[:, c:c + P].reshape(KC, P, P).transpose(1, 0, 2) for c in cols]

    def gate_tile(w, first, second):
        t = np.zeros((D_MODEL, P), f)
        t[:, 0:HEADS] = arr(w)[:, first:first + HEADS]
        t[:, 32:32 + HEADS] = arr(w)[:, second:second + HEADS]
        return t.reshape(KC, P, P).transpose(1, 0, 2)

    def mlp_tiles(layer):
        out = []
        for g in range(GROUPS):
            out += tiles_of(w_up[layer], 0, range(g * D_MODEL, (g + 1) * D_MODEL, P))
            out += tiles_of(w_down[layer], g * D_MODEL, range(0, D_MODEL, P))
        return out

    wa, wc = arr(w_in_a)[0], arr(w_in_c)[0]
    tiles = [gate_tile(wa, 1536, 1540)]
    for h in range(HEADS):
        tiles += tiles_of(wa, 0, [h * P, 512 + h * P, 1024 + h * P, 1544 + h * P])
    for h in range(HEADS):
        tiles += tiles_of(wa, 0, [2056 + h * P, 2568 + h * P, 3080 + h * P, 3592 + h * P])
    tiles += tiles_of(arr(w_out_a)[0], 0, range(0, D_MODEL, P)) + mlp_tiles(0)
    tiles += [gate_tile(wc, 3072, 3076)]
    for h in range(HEADS):
        tiles += tiles_of(wc, 0, [h * P, 512 + h * P] + [1024 + 2 * h * P, 1024 + (2 * h + 1) * P]
                          + [2048 + 2 * h * P, 2048 + (2 * h + 1) * P])
    tiles += tiles_of(arr(w_out_c)[0], 0, range(0, D_MODEL, P)) + mlp_tiles(1)
    assert len(tiles) == TILES
    w_all = np.stack(tiles).reshape(TILES, P, KC * P)

    vec = np.zeros((P, V_ALL), f)
    for name, a in (("mix_a", arr(norm_mix_a)[0]), ("ffn0", arr(norm_ffn)[0]), ("mix_c", arr(norm_mix_c)[0]),
                    ("ffn1", arr(norm_ffn)[1]), ("final", arr(final_gain))):
        vec[:, V_GAIN[name]:V_GAIN[name] + KC] = a.reshape(KC, P).T
    vec[:, V_GDN] = arr(gdn_gain)[0]
    vec[:, V_RET] = arr(ret_gain)[0]
    vec[:, V_ML:V_ML + 2] = arr(mlstm_gain)[0].reshape(2, P).T
    vec[0:HEADS, V_DTB] = arr(dt_bias)[0]
    vec[0:HEADS, V_ALOG] = arr(a_log)[0]
    vec[0:HEADS, V_BI] = arr(b_gate_c)[0, 0:HEADS]
    vec[0:HEADS, V_BF] = arr(b_gate_c)[0, HEADS:]
    vec[:, V_CONV:V_CONV + 48] = arr(w_conv_a)[0].reshape(CONV_W, 12, P).transpose(2, 1, 0).reshape(P, 48)
    vec[0:HEADS, V_M0:V_M0 + NB] = arr(state_mlstm_m)[0].T
    vec[:, V_N0:V_N0 + HEADS * NB] = arr(state_mlstm_n)[0].transpose(2, 1, 0).reshape(P, HEADS * NB)
    vec[:, V_HIST:] = arr(state_conv_a)[0].reshape(NB, 3, 12, P).transpose(3, 2, 1, 0).reshape(P, -1)

    x = np.concatenate([arr(x_prompt)[0], arr(x_sample)[:, 0]]).T.reshape(KC, P, TOK)

    def by_head(st):
        return arr(st)[0].transpose(1, 2, 0, 3).reshape(HEADS, P, -1)

    ins = {"w_all": w_all, "vec": vec, "x": x, "state_a": by_head(state_delta_a), "state_b": by_head(state_ret_b),
           "state_c": by_head(state_mlstm_C), **shape_constants()}
    ins = {k: np.ascontiguousarray(a) for k, a in ins.items()}
    outs = {"y": (KC, P, TOK), "conv_rows": (P, 12 * (3 + 3 * NB)),
            "p_state_a": (HEADS, P, P), "p_state_b": (HEADS, P, P), "p_state_c": (HEADS, P, 2 * P),
            "p_n": (HEADS, P, 1), "p_m": (HEADS, 1),
            "s_state_a": (HEADS, P, NB * P), "s_state_b": (HEADS, P, NB * P), "s_state_c": (HEADS, P, NB * 2 * P),
            "s_n": (HEADS, P, NB), "s_m": (HEADS, NB)}

    nc = bacc.Bacc("TRN2", target_bir_lowering=False, num_devices=1)
    io = {k: nc.dram_tensor(k, a.shape, F32, kind="ExternalInput").ap() for k, a in ins.items()}
    io.update({k: nc.dram_tensor(k, s, F32, kind="ExternalOutput").ap() for k, s in outs.items()})
    io["h_spill"] = nc.dram_tensor("h_spill", (KC, P, TOK), F32, kind="Internal").ap()
    build(nc, io)
    r = run_bass_kernel_spmd(nc, [ins], core_ids=[0]).results[0]

    y = r["y"].reshape(D_MODEL, TOK).T
    conv = r["conv_rows"].reshape(P, 12, 3 + 3 * NB)
    p_conv = conv[:, :, 0:3].transpose(2, 1, 0).reshape(1, 1, 3, 12 * P)
    s_conv = conv[:, :, 3:].reshape(P, 12, 3, NB).transpose(3, 2, 1, 0).reshape(1, NB, 3, 12 * P)

    def samples(a, v):
        return np.ascontiguousarray(a.reshape(HEADS, P, NB, v).transpose(2, 0, 1, 3))[None]

    out = (y[0:SEQ][None], y[SEQ:][:, None], p_conv, r["p_state_a"][None, None], r["p_state_b"][None, None],
           r["p_state_c"][None, None], r["p_n"].reshape(1, 1, HEADS, P), r["p_m"].reshape(1, 1, HEADS),
           s_conv, samples(r["s_state_a"], P), samples(r["s_state_b"], P), samples(r["s_state_c"], 2 * P),
           np.ascontiguousarray(r["s_n"].transpose(2, 0, 1))[None], np.ascontiguousarray(r["s_m"].T)[None])
    return tuple(np.ascontiguousarray(o) for o in out)
```

```python
from contextlib import ExitStack, contextmanager

import numpy as np
import concourse.bass as bass
from concourse import mybir

ALU = mybir.AluOpType
ACT = mybir.ActivationFunctionType
F32 = mybir.dt.float32
F32R = mybir.dt.float32r

P = 128
D_MODEL = 1024
SEQ = 1024
NB = 8
TOK = SEQ + NB
NT = 3
TT = TOK // NT
KC = D_MODEL // P
HEADS = 4
DK = 128
C = 128
NC_ = SEQ // C
LEVELS = 7
CONV_W = 4
D_FF = 4096
GROUPS = D_FF // D_MODEL
EPS = 1e-6
PAST_LEN = 8192
ROPE_BASE = 10000.0
QSCALE = DK ** -0.5

T_AB = 1
T_OUTA = T_AB + 2 * HEADS * 4
T_MLP0 = T_OUTA + KC + 1
T_GC = T_MLP0 + GROUPS * 2 * KC
T_C = T_GC + 1
T_OUTC = T_C + HEADS * 6
T_MLP1 = T_OUTC + KC + 1
TILES = T_MLP1 + GROUPS * 2 * KC

KTAIL = (1, 2)
PARTIAL = ((3, 0, 1, 2), (4, 5, 2, 3))
ORDER = ((4, 3, 0, 5, 1, 6, 2, 7), (0, 4, 5, 1, 2, 6, 3, 7))
HI_BY_ACT = 2
IN_TURN = tuple(range(KC))

DELTA_FILL = {"start": 7, "conv q": 14, "conv k": 10, "conv v": 8, "norm": 4, "operands": 12, "invert": 2,
              "level 0": 0, "level 1": 0, "block": 0, "turn": 0, "scan": 1, "state": 1, "residual": 1, "values": 1,
              "sample": 2, "rows": 3, "output": 3, "outer": 0}
RETENTION_FILL = {"gate": 5, "rope q": 10, "rope k": 10, "operands": 10, "scan": 8,
                  "state": 4, "sample": 4, "rows": 5, "outer": 3, "output": 5}
RETENTION_LAST_FILL = {**RETENTION_FILL, "state": 2, "output": 6}
MLSTM_FILL = {"start": 7, "gate 0": 8, "gate 1": 8, "operands": 6, "scan": 8,
              "state": 5, "den": 6, "sample": 6, "rows": 9, "output": 10, "outer": 5}
MLSTM_LAST_FILL = {"start": 4, "gate 0": 4, "gate 1": 4, "operands": 4, "scan": 4,
                   "state": 3, "den": 3, "sample": 3, "rows": 7, "outer": 2, "output": 8}
SHORT_STEPS = ("sample", "rows")

V_GAIN = {"mix_a": 0, "ffn0": 8, "mix_c": 16, "ffn1": 24, "final": 32}
V_GDN, V_RET, V_ML = 40, 41, 42
V_DTB, V_ALOG, V_BI, V_BF = 44, 45, 46, 47
V_CONV = 48
V_M0 = V_CONV + 48
V_N0 = V_M0 + NB
V_HIST = V_N0 + HEADS * NB
V_ALL = V_HIST + 12 * 3 * NB
K_ID, K_ONE, K_CAUS = 0, P, 2 * P
K_RG = 3 * P
K_RK = K_RG + 8
K_ALL = K_RK + 4


TAILS = (T_OUTA, T_OUTC)


def w_slot(t):
    return (t - sum(tail < t for tail in TAILS)) % 2


class Tally:

    def __init__(self, eng, step):
        self.eng, self.step = eng, step
        self.n, self.names, self.last = {}, {}, None
        self.i, self.per = None, {}

    def _value(self, key):
        value = self.n[key]
        if self.i is not None and self.per.get(key):
            value = self.i * self.per[key] + value
        return value

    def made(self, sem):
        key = sem.name
        self.n[key] = self.n.get(key, 0) + 1
        self.last = (sem, key)
        self.at = self._value(key)
        return sem, 1

    def stepped(self):
        return self.made(self.step)

    def settle(self):
        self.eng.wait_ge(self.last[0], self.at)

    def awaited(self, sem, by=1):
        key = "w " + sem.name
        self.n[key] = self.n.get(key, 0) + by
        return sem, self._value(key)

    @contextmanager
    def loop(self, count, per):
        start = dict(self.n)
        with self.eng.Fori(0, count) as i:
            self.i, self.per = i, per
            yield i
            self.i, self.per = None, {}
        for key, value in self.n.items():
            turn = value - start.get(key, 0)
            assert turn == per.get(key, 0), (key, turn, per.get(key, 0))
            self.n[key] = start.get(key, 0) + count * turn
        if self.last:
            self.at = self.n[self.last[1]]


def build(nc, io):
    with ExitStack() as ctx:
        def sem(name):
            return ctx.enter_context(nc.semaphore(name))

        base = (nc.sbuf_base + 31) // 32 * 32
        cursor = [base]

        def place(name, shape, dtype=F32, at=None):
            size = int(np.prod(shape[1:])) * 4
            if at is None:
                at = cursor[0]
                cursor[0] += (size + 31) // 32 * 32
            return nc.alloc_sbuf_tensor_at(name, list(shape), dtype, offset=at)

        R = TOK * 4
        raw = [place(f"w_raw{s}", [P, KC, P]) for s in range(2)]
        w_hi = [place(f"w_hi{s}", [P, KC, P], F32R) for s in range(2)]
        w_lo = [place(f"w_lo{s}", [P, KC, P], F32R) for s in range(2)]
        region = []
        ops = []
        for s in range(2):
            region.append(cursor[0])
            ops.append((place(f"x_hi{s}", [P, KC, TOK], F32R), place(f"x_lo{s}", [P, KC, TOK], F32R)))
        h_at = cursor[0]
        H = place("h", [P, KC, TOK])
        MIX = place("mix", [P, KC, TOK], at=h_at)
        extra = cursor[0]
        SSQ = place("ssq", [P, TOK])
        SQT = place("sq_third", [P, TOK])
        consts = place("consts", [P, K_ALL])
        vec = place("vec", [P, V_ALL])
        rbc = place("rbc", [P, TOK])
        gcol = place("gate_cols", [P, NC_, 36])
        negbe = place("neg_beta_eg", [P, NC_, HEADS])
        convo = place("conv_out_rows", [P, 12, 3 + 3 * NB])
        S = place("state", [P, 2 * P + 1])
        resid = place("v_resid", [P, P])
        vnew = place("v_new", [P, P])
        small = place("small", [P, 12 * NB])
        samp = place("sample_qkv", [P, 4 * NB])
        kq = place("kq_sample", [P, NB, 2])
        krow = place("k_rows", [NB, P])
        vrow = place("v_rows", [NB, 2 * P])
        eps = place("eps", [P, 4])
        negea = place("neg_exp_a", [P, 1])
        one = place("one", [P, KC])
        assert cursor[0] <= nc.sbuf_usable_end, (cursor[0], nc.sbuf_usable_end)
        T_third = place("mlp_t", [P, TT], at=extra)
        U_third = place("mlp_u", [P, TT], at=extra + TT * 4)

        slots = []
        for layer in range(2):
            r0 = region[1 - layer]
            slots.append([place(f"s{layer}_{i}", [P, TOK], at=r0 + i * R) for i in range(16)]
                         + [place(f"s{layer}_{16 + i}", [P, TOK], at=extra + i * R) for i in range(2)])
        tail_w = [(place("tail_hi0", [P, 4, P], F32R, at=region[1] + 15 * R),
                   place("tail_lo0", [P, 4, P], F32R, at=region[1] + 15 * R + 4 * P * 4)),
                  (place("tail_hi1", [P, 8, P], F32R, at=region[0] + 7 * R),
                   place("tail_lo1", [P, 8, P], F32R, at=region[0] + 15 * R))]
        ss_c = place("sample_C", [P, NB, 2 * P], at=region[0] + 8 * R)
        levels = place("levels", [P, LEVELS + 1, P // 2], at=h_at + 6 * R)
        rows_a = place("gate_rows_a", [P, TOK], at=h_at + 7 * R)
        rows_c = place("gate_rows_c", [P, TOK], at=h_at + 7 * R)

        ident, ones, causal = (consts[:, k:k + P] for k in (K_ID, K_ONE, K_CAUS))

        PJ = ctx.enter_context(nc.psum_tensor("proj", [P, NT, 512], F32))
        MB = [ctx.enter_context(nc.psum_tensor(f"bank{b}", [P, 512], F32)) for b in range(5)]

        w_loaded = [sem("w_loaded0"), sem("w_loaded1")]
        w_one, w_hi_done, w_split = sem("w_one"), sem("w_hi_done"), sem("w_split")
        proj_full, proj_drained = sem("proj_full"), sem("proj_drained")
        x_ready = sem("x_ready")
        mix_hi, h_added, rows_stored = sem("mix_hi"), sem("h_added"), sem("rows_stored")
        sq_made, ssq_added, rbc_ready = sem("sq_made"), sem("ssq_added"), sem("rbc_ready")
        consts_in, h_in = sem("consts_in"), [sem(f"h_in{i}") for i in range(KC)]
        h_spilled, mask_in, bconst_in = sem("h_spilled"), sem("mask_in"), sem("bconst_in")
        state_in, state_final, stored = sem("state_in"), sem("state_final"), sem("stored")
        dve_step, act_step = sem("dve_step"), sem("act_step")
        setup_done = sem("setup_done")
        to_act, to_dve, to_pe = sem("to_act"), sem("to_dve"), sem("to_pe")
        act_to_pe = sem("act_to_pe")
        y_done = sem("y_done")
        full = {r: [sem(f"full_{r}{b}") for b in range(5)] for r in ("dve", "act")}
        drained = {r: [sem(f"drained_{r}{b}") for b in range(5)] for r in ("dve", "act")}

        def third(a, tt):
            return a[:, tt * TT:(tt + 1) * TT]

        def chunk(a, c, n=1):
            return a[:, c * C:(c + n) * C]

        def rep(a, n):
            return a.unsqueeze(1).broadcast_to([a.shape[0], n, a.shape[1]])

        def spread(a, m):
            return a.unsqueeze(2).broadcast_to([a.shape[0], a.shape[1], m])

        def every_other(a, lv, which):
            return a.rearrange("p (n two b) -> p n two b", two=2, b=1 << lv)[:, :, which, :]

        def cut(a, n):
            return a.rearrange("p (n m) -> p n m", n=n)

        XR = {"mix0": 24, "xg1": 48, "hid0": 72, "xg2": 168, "mix1": 192, "xg3": 216, "hid1": 240}
        block = ctx.enter_context(nc.Block())

        @block.sync
        def _(sp):
            sp.dma_start(raw[0][:], io["w_all"][0]).then_inc(w_loaded[0], 16)
            for c in range(KC):
                sp.dma_start(H[:, c, :], io["x"][c]).then_inc(h_in[c], 16)
                if c == 2:
                    sp.dma_start(raw[1][:], io["w_all"][1]).then_inc(w_loaded[1], 16)
            with sp.Fori(0, TILES // 2 - 1) as i:
                for s in range(2):
                    sp.wait_ge(w_split, 2 * i + s + 1)
                    sp.dma_start(raw[s][:], io["w_all"][2 * i + 2 + s]).then_inc(w_loaded[s], 16)

        @block.gpsimd
        def _(pool):
            def split(t, i, free, to=None):
                chunks = KC if to is None else to[0].shape[1]
                hi, lo = to or (w_hi[w_slot(t)], w_lo[w_slot(t)])
                src = raw[t % 2][:, 0:chunks, :]
                pool.wait_ge(w_loaded[t % 2], 16 * i + 16 * (t // 2 + 1))
                if free is not None:
                    pool.wait_ge(proj_full, free)
                nc.gpsimd.tensor_tensor(hi[:], src, one[:, 0:chunks].unsqueeze(2).broadcast_to([P, chunks, P]),
                                        ALU.mult).then_inc(w_hi_done, 1)
                pool.wait_ge(w_hi_done, 2 * i + t + 1)
                nc.gpsimd.tensor_tensor(lo[:], src, hi[:].bitcast(F32), ALU.subtract).then_inc(w_split, 1)

            def run(t0, t1):
                with pool.Fori(0, (t1 - t0) // 2) as i:
                    for t in (t0, t0 + 1):
                        split(t, i, 6 * i + 3 * t - 3)
                if (t1 - t0) % 2:
                    split(t1 - 1, 0, 3 * t1 - 6)

            nc.gpsimd.memset(one[:], 1.0).then_inc(w_one, 1)
            pool.wait_ge(w_one, 1)
            for t in range(2):
                split(t, 0, None)
            for c in range(1, KC):
                for tt in range(NT):
                    pool.wait_ge(sq_made, 3 * c + tt + 1)
                    if c > 1:
                        pool.wait_ge(ssq_added, 3 * (c - 2) + tt + 1)
                    nc.gpsimd.tensor_tensor(third(SSQ, tt), third(SSQ, tt), third(SQT, tt), ALU.add).then_inc(ssq_added, 1)
            t = 2
            for layer, tail in enumerate(TAILS):
                run(t, tail)
                split(tail, 0, 3 * tail - 3, tail_w[layer])
                for t in (tail + 1, tail + 2):
                    split(t, 0, 3 * t - 6)
                t = tail + 3
            run(t, TILES)

        @block.tensor
        def _(pe):
            n = Tally(pe, None)
            owner = [None] * 5

            def claim(b, reader):
                if owner[b]:
                    pe.wait_ge(drained[owner[b]][b], n.n["f" + owner[b] + str(b)])
                owner[b] = reader

            def publish(ins, b):
                key = "f" + owner[b] + str(b)
                n.n[key] = n.n.get(key, 0) + 1
                ins.then_inc(full[owner[b]][b], 1)

            def tile(t, slot, X, ready=None, order=IN_TURN, thirds=None):
                for _ in tile_steps(t, slot, X, ready, order, thirds):
                    pass

            def tile_steps(t, slot, X, ready=None, order=IN_TURN, thirds=None):
                hi, lo = X
                pe.wait_ge(w_split, t + 1)
                for tt in range(NT):
                    if thirds:
                        pe.wait_ge(x_ready, thirds[tt])
                    pe.wait_ge(proj_drained, 3 * t + tt - 2)
                    for at, k in enumerate(order):
                        if ready is not None:
                            pe.wait_ge(x_ready, ready + 3 * at + tt + 1)
                        for j, (w, x) in enumerate(((w_hi, hi), (w_hi, lo), (w_lo, hi))):
                            last = nc.tensor.matmul(PJ[:, tt, 0:TT], w[slot][:, k, :],
                                                    x[:, k, tt * TT:(tt + 1) * TT],
                                                    start=(at == 0 and j == 0),
                                                    stop=(at == len(order) - 1 and j == 2))
                        if at == len(order) - 1:
                            last.then_inc(proj_full, 1)
                        yield

            def first_tile(X):
                hi, lo = X
                pe.wait_ge(w_split, 1)
                for k in range(KC):
                    for tt in range(NT):
                        pe.wait_ge(x_ready, 3 * k + tt + 1)
                        for j, (w, x) in enumerate(((w_hi, hi), (w_hi, lo), (w_lo, hi))):
                            last = nc.tensor.matmul(PJ[:, tt, 0:TT], w[0][:, k, :], x[:, k, tt * TT:(tt + 1) * TT],
                                                    start=(k == 0 and j == 0), stop=(k == KC - 1 and j == 2))
                        if k == KC - 1:
                            last.then_inc(proj_full, 1)

            def norm_finish(number):
                pe.wait_ge(ssq_added, 21 * (number + 1))
                for tt in range(NT):
                    claim(tt, "act")
                    publish(nc.tensor.matmul(MB[tt][:, 0:TT], ones, third(SSQ, tt), start=True, stop=True), tt)

            def over_partitions(lhs, src, reader):
                for tt in range(NT):
                    claim(tt, reader)
                    publish(nc.tensor.matmul(MB[tt][:, 0:TT], lhs, third(src, tt), start=True, stop=True), tt)

            def per_chunk(b, reader, half, f):
                claim(b, reader)
                for q in range(4):
                    last = f(MB[b][:, q * C:(q + 1) * C], 4 * half + q)
                publish(last, b)

            def turned(b, reader, src, half):
                per_chunk(b, reader, half, lambda o, c: nc.tensor.transpose(o, chunk(src, c), ident))

            def mm(o, l, r, start=True, stop=True):
                return nc.tensor.matmul(o, l, r, start=start, stop=stop)

            def sel(row, rows):
                return consts[0:rows, K_ID + row:K_ID + row + 1].broadcast_to([rows, P])

            def sample_outer(values):
                pe.wait_ge(*n.awaited(to_pe))
                claim(4, "dve")
                nc.tensor.transpose(MB[4][0:NB, 0:P], small[:, 0:NB], ident)
                for j, v in enumerate(values):
                    last = nc.tensor.transpose(MB[4][0:NB, (j + 1) * P:(j + 2) * P], v, ident)
                publish(last, 4)

            def mixer_ab(s, h, delta):
                if delta:
                    over_partitions(sel(32 + h, 36), rows_a[0:36, :], "act")
                    yield "start"
                    over_partitions(sel(h, 36), rows_a[0:36, :], "dve")
                    yield "conv q"
                    yield "conv k"
                    yield "conv v"
                    for x in (10, 12):
                        yield "norm"
                        pe.wait_ge(*n.awaited(act_to_pe))
                        over_partitions(ones, s[x], "act")
                else:
                    yield "gate"
                    yield "rope q"
                    yield "rope k"
                q, k, v = (s[4], s[5], s[6]) if delta else (s[6], s[7], s[2])
                yield "operands"
                pe.wait_ge(*n.awaited(to_pe))
                for half in range(2):
                    turned(half, "dve", k, half)
                for half in range(2):
                    turned(2 + half, "dve", v, half)
                if delta:
                    for half in range(2):
                        per_chunk((4, 0)[half], "dve", half, lambda o, c: mm(o, chunk(k, c), chunk(s[14], c)))
                for half in range(2):
                    per_chunk(1 + half, "dve", half, lambda o, c: mm(o, chunk(k, c), chunk(q, c)))
                if delta:
                    LT, Pm, Dm, E = s[12], s[11], s[14], s[15]
                    for half in range(2):
                        yield "invert"
                        pe.wait_ge(*n.awaited(to_pe))
                        turned(half, "dve", LT, half)
                    for lv in range(1, LEVELS):
                        for half in range(2):
                            yield f"level {half}"
                            pe.wait_ge(*n.awaited(to_pe))
                            per_chunk(half, "dve", half, lambda o, c: mm(o, chunk(LT, c), chunk(Dm, c)))
                        for half in range(2):
                            yield "block"
                            pe.wait_ge(*n.awaited(to_pe))
                            per_chunk((3, half)[half], "dve", half, lambda o, c: mm(o, chunk(Pm, c), chunk(E, c)))
                        if lv < LEVELS - 1:
                            for half in range(2):
                                yield "turn"
                                pe.wait_ge(*n.awaited(to_pe))
                                turned((2, 4)[half], "dve", E, half)
                Kd, V, qg, QKT = s[16], s[17], s[10], s[13]
                yield "scan"
                pe.wait_ge(*n.awaited(to_pe))
                for c in range(NC_):
                    if c:
                        yield "state"
                        pe.wait_ge(*n.awaited(to_pe))
                    if delta:
                        claim(0, "dve")
                        publish(mm(MB[0][:, 0:P], chunk(k, c), S[:, 0:P]), 0)
                    claim(2, "act")
                    mm(MB[2][:, 0:C], S[:, 0:P], chunk(qg, c), True, False)
                    if delta:
                        yield "residual"
                        pe.wait_ge(*n.awaited(to_pe))
                        claim(1, "dve")
                        publish(mm(MB[1][:, 0:P], chunk(s[15], c), resid[:]), 1)
                        yield "values"
                        pe.wait_ge(*n.awaited(to_pe))
                    vv = vnew[:] if delta else chunk(V, c)
                    publish(mm(MB[2][:, 0:C], vv, chunk(QKT, c), False, True), 2)
                    claim(3, "dve")
                    publish(mm(MB[3][:, 0:P], chunk(Kd, c), vv), 3)
                yield "sample"
                pe.wait_ge(*n.awaited(to_pe))
                pe.wait_ge(state_in, n.awaited(state_in, 16)[1])
                claim(4, "dve")
                for b in range(NB):
                    mm(MB[4][:, 2 * b:2 * b + 2], s[9][:, b * P:(b + 1) * P], kq[:, b, :])
                publish(mm(MB[4][:, 2 * NB:3 * NB], ones, small[:, 0:NB]), 4)
                yield "rows"
                sample_outer([small[:, NB:2 * NB] if delta else samp[:, 0:NB]])
                yield "output"
                pe.wait_ge(*n.awaited(act_to_pe))
                over_partitions(ones, s[12], "act")
                yield "outer"
                pe.wait_ge(*n.awaited(to_pe))
                for half in range(2):
                    b = (3, 0)[half]
                    claim(b, "dve")
                    publish(mm(MB[b][:], krow[0:NB, :], s[13][0:NB, half * 512:(half + 1) * 512]), b)

            def mixer_c(s, h):
                over_partitions(sel(h, 100), rows_c[0:100, :], "dve")
                claim(3, "dve")
                mm(MB[3][:, NB:2 * NB], sel(64 + h, 100), rows_c[0:100, SEQ:TOK])
                publish(mm(MB[3][:, 0:NB], sel(96 + h, 100), rows_c[0:100, SEQ:TOK]), 3)
                yield "start"
                over_partitions(sel(32 + h, 100), rows_c[0:100, :], "act")
                q, k = s[0], s[1]
                yield "gate 0"
                yield "gate 1"
                yield "operands"
                pe.wait_ge(*n.awaited(to_pe))
                for half in range(2):
                    turned(half, "dve", k, half)
                for half in range(2):
                    turned(2 + half, "dve", s[2], half)
                for half in range(2):
                    turned((4, 0)[half], "dve", s[3], half)
                for half in range(2):
                    per_chunk(1 + half, "dve", half, lambda o, c: mm(o, chunk(k, c), chunk(q, c)))
                Kd, V0, V1, qw, QKW = s[16], s[17], s[13], s[10], s[11]
                yield "scan"
                pe.wait_ge(*n.awaited(to_pe))
                for c in range(NC_):
                    if c:
                        yield "state"
                        pe.wait_ge(*n.awaited(to_pe))
                    for j, v in enumerate((chunk(V0, c), chunk(V1, c))):
                        claim(j, "act")
                        mm(MB[j][:, 0:C], S[:, j * P:(j + 1) * P], chunk(qw, c), True, False)
                        publish(mm(MB[j][:, 0:C], v, chunk(QKW, c), False, True), j)
                    if c == 0:
                        claim(2, "dve")
                    mm(MB[2][:, c:c + 1], chunk(qw, c), S[:, 2 * P:2 * P + 1], True, False)
                    last = mm(MB[2][:, c:c + 1], chunk(QKW, c), ones[:, 0:1], False, True)
                    if c == NC_ - 1:
                        publish(last, 2)
                    claim(3, "dve")
                    for j, v in enumerate((chunk(V0, c), chunk(V1, c), ones[:, 0:1])):
                        last = mm(MB[3][:, j * P:j * P + v.shape[1]], chunk(Kd, c), v)
                    publish(last, 3)
                yield "den"
                pe.wait_ge(*n.awaited(to_pe))
                for half in range(2):
                    per_chunk(2 + half, "dve", half,
                              lambda o, c: mm(o, small[:, 11 * NB + c:11 * NB + c + 1].broadcast_to([P, P]), ident))
                yield "sample"
                pe.wait_ge(*n.awaited(to_pe))
                pe.wait_ge(state_in, n.awaited(state_in, 16)[1])
                claim(4, "dve")
                for b in range(NB):
                    for j in range(2):
                        mm(MB[4][:, j * NB + b:j * NB + b + 1], ss_c[:, b, j * P:(j + 1) * P], samp[:, b:b + 1])
                mm(MB[4][:, 2 * NB:3 * NB], ones, small[:, 0:NB])
                publish(mm(MB[4][:, 3 * NB:4 * NB], ones, small[:, NB:2 * NB]), 4)
                yield "rows"
                sample_outer([samp[:, 2 * NB:3 * NB], samp[:, 3 * NB:4 * NB]])
                yield "output"
                pe.wait_ge(*n.awaited(act_to_pe))
                for tt in range(NT):
                    claim(tt, "act")
                    mm(MB[tt][:, 0:TT], ones, third(s[10], tt), True, False)
                    publish(mm(MB[tt][:, 0:TT], ones, third(s[11], tt), False, True), tt)
                for j in range(2):
                    yield "outer"
                    pe.wait_ge(*n.awaited(to_pe))
                    for half in range(2):
                        b = (3, 0)[half]
                        claim(b, "dve")
                        publish(mm(MB[b][:], krow[0:NB, :], s[13][0:NB, half * 512:(half + 1) * 512]), b)

            def out_partial(layer, t0, X, ready):
                pe.wait_ge(proj_drained, 3 * t0 + 3)
                pe.sem_inc(proj_full, 3)
                for j in range(4):
                    t = t0 + 1 + j
                    yield from tile_steps(t, w_slot(t), X, ready if j == 0 else None,
                                          order=IN_TURN[:KC - KTAIL[layer]])

            def out_rest(layer, t0, X, ready):
                hi, lo = X
                thi, tlo = tail_w[layer]
                t, kt = t0 + 5, KTAIL[layer]
                split = [ready + 3 * (KC - kt) + kt * (tt + 1) for tt in range(NT)]
                for chunk_ in ORDER[layer]:
                    if chunk_ not in PARTIAL[layer]:
                        tile(t, w_slot(t), X, thirds=split if chunk_ == ORDER[layer][0] else None)
                        t += 1
                        continue
                    n0 = PARTIAL[layer].index(chunk_)
                    for tt in range(NT):
                        claim(tt, "dve")
                        for k in range(kt):
                            for j, (w, x) in enumerate(((thi, hi), (thi, lo), (tlo, hi))):
                                last = nc.tensor.matmul(MB[tt][:, 0:TT], w[:, k * 4 + n0, :],
                                                        x[:, KC - kt + k, tt * TT:(tt + 1) * TT],
                                                        start=(k == 0 and j == 0), stop=(k == kt - 1 and j == 2))
                        publish(last, tt)

            def mlp(t0, X, Y, ready, hid, order):
                with n.loop(GROUPS - 1, {}) as g:
                    for k in range(KC):
                        tile(t0 + 16 * g + k, w_slot(t0 + k), X, ready if k == 0 else None, order=order)
                    for k in range(KC):
                        tile(t0 + 16 * g + 8 + k, w_slot(t0 + 8 + k), Y, hid + 24 * g if k == 0 else None)
                g = GROUPS - 1
                for k in range(KC):
                    tile(t0 + 16 * g + k, w_slot(t0 + k), X)
                for k in range(KC):
                    tile(t0 + 16 * g + 8 + k, w_slot(t0 + 8 + k), Y, hid + 24 * g if k == 0 else None)

            def rows_turned(rows, count):
                pe.wait_ge(*n.awaited(to_pe))
                for half in range(2):
                    claim(half, "dve")
                    for q in range(4):
                        last = nc.tensor.transpose(MB[half][:, q * count:(q + 1) * count],
                                                   rows[0:count, (4 * half + q) * C:(4 * half + q + 1) * C],
                                                   consts[0:count, K_ID:K_ID + count])
                    publish(last, half)

            def projections(t0, count, X):
                for t in range(t0, t0 + count):
                    yield from tile_steps(t, w_slot(t), X)

            def weave(mixer, following, fill):
                for place in mixer:
                    for _ in range(fill[place]):
                        next(following, None)
                for _ in following:
                    pass

            XA, XB = ops
            pe.wait_ge(setup_done, 1)
            pe.wait_ge(consts_in, 32)
            first_tile(XA)
            norm_finish(0)
            for _ in projections(T_AB, 4, XA):
                pass
            rows_turned(rows_a, 36)
            for u in range(2 * HEADS):
                mixer = mixer_ab(slots[0], u % HEADS, u < HEADS)
                following = (projections(T_AB + 4 * u + 4, 4, XA) if u < 2 * HEADS - 1
                             else out_partial(0, T_OUTA, XA, XR["mix0"]))
                weave(mixer, following, DELTA_FILL if u < HEADS else RETENTION_FILL if u < 2 * HEADS - 1
                      else RETENTION_LAST_FILL)
            out_rest(0, T_OUTA, XA, XR["mix0"])
            norm_finish(1)
            mlp(T_MLP0, XB, XA, XR["xg1"], XR["hid0"], ORDER[0])
            tile(T_GC, w_slot(T_GC), XB, XR["xg2"])
            norm_finish(2)
            for _ in projections(T_C, 6, XB):
                pass
            rows_turned(rows_c, 100)
            for u in range(HEADS):
                following = (projections(T_C + 6 * u + 6, 6, XB) if u < HEADS - 1
                             else out_partial(1, T_OUTC, XB, XR["mix1"]))
                weave(mixer_c(slots[1], u), following, MLSTM_FILL if u < HEADS - 1 else MLSTM_LAST_FILL)
            out_rest(1, T_OUTC, XB, XR["mix1"])
            norm_finish(3)
            mlp(T_MLP1, XA, XB, XR["xg3"], XR["hid1"], ORDER[1])
            norm_finish(4)

        @block.vector
        def _(v):
            n = Tally(v, dve_step)
            tt_, ts_, stt = nc.vector.tensor_tensor, nc.vector.tensor_scalar, nc.vector.scalar_tensor_tensor

            def take(b):
                v.wait_ge(*n.awaited(full["dve"][b]))
                return MB[b]

            def done(b):
                return n.made(drained["dve"][b])

            def step(ins):
                ins.then_inc(*n.stepped())
                n.settle()

            def tell(sem):
                n.settle()
                v.sem_inc(*n.made(sem))

            def drain(t, tt, f):
                v.wait_ge(proj_full, 3 * t + tt + 1)
                f(PJ[:, tt, 0:TT], tt).then_inc(proj_drained, 1)

            def vcol(k):
                return vec[:, k:k + 1]

            def norm_chunk(c, at, tt, number, gain, X, hi_by_act=False):
                hh = H[:, c, tt * TT:(tt + 1) * TT]
                if hi_by_act:
                    v.wait_ge(*n.awaited(sq_made))
                if X is not None:
                    hi, lo = (x[:, c, tt * TT:(tt + 1) * TT] for x in X)
                    if not hi_by_act:
                        step(ts_(hi, hh, vcol(gain + c), None, ALU.mult))
                    stt(lo, hh, vcol(gain + c), hi.bitcast(F32), ALU.mult, ALU.subtract).then_inc(x_ready, 1)
                if not hi_by_act:
                    v.wait_ge(*n.awaited(sq_made))
                if at:
                    tt_(third(SSQ, tt), third(SSQ, tt), third(SQT, tt), ALU.add).then_inc(ssq_added, 1)
                    v.wait_ge(ssq_added, 21 * number + 3 * (at - 1) + tt + 1)

            def project(t, dst, scale=None):
                for _ in project_steps(t, dst, scale):
                    pass

            def project_steps(t, dst, scale=None):
                def f(ps, tt):
                    if scale is None:
                        return tt_(third(dst, tt), ps, third(rbc, tt), ALU.mult)
                    return stt(third(dst, tt), ps, scale, third(rbc, tt), ALU.mult, ALU.mult)
                for tt in range(NT):
                    drain(t, tt, f)
                    yield

            def projections(s, t0, u, count):
                order = (3, 0, 1, 2) if count == 4 else (4, 5, 2, 3, 0, 1)
                for j in range(count):
                    yield from project_steps(t0 + count * u + j, s[order[j]], QSCALE if (count, order[j]) == (6, 1) else None)

            def weave(mixer, following, fill, per=KC):
                steps = thirds = 0
                for place in mixer:
                    steps += fill[place]
                    if place not in SHORT_STEPS:
                        for _ in range(steps // per - thirds):
                            next(following, None)
                        thirds = steps // per
                for _ in following:
                    pass

            def all_drained(t):
                v.wait_ge(proj_drained, 3 * t + 3)

            def residual(t, c, at, number, gain, X):
                for tt in range(NT):
                    hh = H[:, c, tt * TT:(tt + 1) * TT]
                    drain(t, tt, lambda ps, tt: tt_(hh, hh, ps, ALU.add))
                    v.wait_ge(proj_drained, 3 * t + tt + 1)
                    norm_chunk(c, at, tt, number, gain, X)

            def out_start(layer, X):
                v.sem_inc(proj_drained, 3)
                for c in range(KC - KTAIL[layer]):
                    v.wait_ge(*n.awaited(mix_hi))
                    for tt in range(NT):
                        hi, lo = (x[:, c, tt * TT:(tt + 1) * TT] for x in X)
                        tt_(lo, MIX[:, c, tt * TT:(tt + 1) * TT], hi.bitcast(F32), ALU.subtract).then_inc(x_ready, 1)

            def out_partial(s, layer, t0):
                for j in range(4):
                    dst = s[PARTIAL[layer][j]]
                    for tt in range(NT):
                        drain(t0 + 1 + j, tt, lambda ps, tt: nc.vector.tensor_copy(third(dst, tt), ps))
                        yield

            def out_rest(s, layer, t0, number, gain, X, loads):
                t = t0 + 5
                before = None
                for at, c in enumerate(ORDER[layer]):
                    v.wait_ge(h_in[c], 16 * loads)
                    for tt in range(NT):
                        hh = H[:, c, tt * TT:(tt + 1) * TT]
                        if c not in PARTIAL[layer]:
                            drain(t, tt, lambda ps, tt: tt_(hh, hh, ps, ALU.add))
                        else:
                            ps, part = take(tt), third(s[c], tt)
                            tt_(part, part, ps[:, 0:TT], ALU.add).then_inc(*done(tt))
                            n.settle()
                            tt_(hh, hh, part, ALU.add).then_inc(*n.made(h_added))
                        if before:
                            norm_chunk(*before, number, gain, X, hi_by_act=True)
                        before = c, at, tt
                    t += c not in PARTIAL[layer]
                norm_chunk(*before, number, gain, X, hi_by_act=True)

            def mix_split(X, layer, tt):
                if tt >= 0:
                    for c in range(KC - KTAIL[layer], KC):
                        hi, lo = (x[:, c, tt * TT:(tt + 1) * TT] for x in X)
                        m = MIX[:, c, tt * TT:(tt + 1) * TT]
                        v.wait_ge(*n.awaited(mix_hi))
                        tt_(lo, m, hi.bitcast(F32), ALU.subtract).then_inc(x_ready, 1)

            def sample_outer(vm, j):
                step(tt_(cut(vm[0:NB, 0:NB * P], NB), rep(vrow[0:NB, j * P:(j + 1) * P], NB),
                         spread(consts[0:NB, K_ID:K_ID + NB], P), ALU.mult))

            def mixer_ab(s, h, delta, unit):
                def gate():
                    v.wait_ge(*n.awaited(to_dve))
                    step(stt(MIX[:, unit, :], s[16][:], 1.0, s[3][:], ALU.add, ALU.mult))

                def conv(x):
                    blk = x * HEADS + h
                    src, dst = s[x], s[4 + x]
                    w = V_CONV + 4 * blk
                    if x == 0:
                        step(ts_(dst[:], src[:], vcol(w + 3), None, ALU.mult))
                    elif x == 1:
                        v.wait_ge(*n.awaited(to_dve))
                    for i in range(3):
                        sh = 3 - i
                        hist = vec[:, V_HIST + (3 * blk + i) * NB:V_HIST + (3 * blk + i + 1) * NB]
                        stt(dst[:, SEQ:TOK], hist, vcol(w + i), dst[:, SEQ:TOK], ALU.mult, ALU.add).then_inc(*n.stepped())
                        step(stt(dst[:, sh:SEQ], src[:, 0:SEQ - sh], vcol(w + i), dst[:, sh:SEQ], ALU.mult, ALU.add))
                    nc.vector.tensor_copy(convo[:, blk, 0:3], src[:, SEQ - 3:SEQ])
                    nc.vector.tensor_copy(convo[:, blk, 3:3 + 2 * NB],
                                          vec[:, V_HIST + (3 * blk + 1) * NB:V_HIST + (3 * blk + 3) * NB])
                    nc.vector.tensor_copy(convo[:, blk, 3 + 2 * NB:], src[:, SEQ:TOK]).then_inc(*n.made(to_act))

                def silu(x):
                    v.wait_ge(*n.awaited(to_dve))
                    return stt(s[4 + x][:], (s[10], s[12], s[13])[x][:], 1.0, s[4 + x][:], ALU.add, ALU.mult)

                if delta:
                    yield "start"
                    conv(0)
                    gate()
                    for tt in range(NT):
                        ps = take(tt)
                        nc.vector.tensor_copy(third(s[7], tt), ps[:, 0:TT]).then_inc(*done(tt))
                    n.settle()
                    for c in range(NC_):
                        last = ts_(chunk(s[11], c), chunk(s[7], c), gcol[:, c, h:h + 1], 0.0, ALU.subtract, ALU.min)
                    last.then_inc(*n.made(to_act))
                    silu(0).then_inc(*n.made(to_act))
                    yield "conv q"
                    conv(1)
                    v.wait_ge(*n.awaited(to_dve))
                    step(tt_(cut(s[11][:, 0:SEQ], NC_), cut(s[11][:, 0:SEQ], NC_), rep(causal, NC_), ALU.mult))
                    silu(1).then_inc(*n.made(to_act))
                    yield "conv k"
                    conv(2)
                    step(silu(2))
                    yield "conv v"
                    yield "norm"
                    yield "norm"
                    v.wait_ge(*n.awaited(to_dve))
                    step(stt(s[4][:], s[4][:], QSCALE, s[10][:], ALU.mult, ALU.mult))
                    step(tt_(s[10][:], s[4][:], s[7][:], ALU.mult))
                    v.wait_ge(*n.awaited(to_dve))
                    step(tt_(s[5][:], s[5][:], s[12][:], ALU.mult))
                    tt_(s[14][:], s[5][:], s[8][:], ALU.mult).then_inc(*n.made(to_pe))
                    q, k, vs, OT = s[4], s[5], s[6][:, SEQ:TOK], s[6]
                else:
                    if h == 0:
                        v.wait_ge(bconst_in, 48)
                    gate()
                    yield "gate"
                    cos, sin = s[4], s[5]
                    for x in range(2):
                        rot = s[(12, 14)[x]]
                        v.wait_ge(*n.awaited(to_dve))
                        sc = 1.0 if x == 0 else QSCALE
                        step(stt(s[6 + x][:], s[x][:], sc, cos[:], ALU.mult, ALU.mult))
                        step(stt(rot[:], rot[:], sc, sin[:], ALU.mult, ALU.mult))
                        step(tt_(s[6 + x][:], s[6 + x][:], rot[:], ALU.add))
                        yield ("rope q", "rope k")[x]
                    nc.vector.tensor_copy(samp[:, 0:NB], s[2][:, SEQ:TOK])
                    eg = s[8][:, 512 + h * P:512 + (h + 1) * P]
                    tt_(cut(s[10][:, 0:SEQ], NC_), cut(s[6][:, 0:SEQ], NC_), rep(eg, NC_), ALU.mult).then_inc(*n.made(to_pe))
                    q, k, vs, OT = s[6], s[7], samp[:, 0:NB], s[11]
                yield "operands"
                for half in range(2):
                    ps = take(half)
                    o = cut(chunk(s[16], 4 * half, 4), 4)
                    if delta:
                        tt_(o, cut(ps[:], 4), cut(chunk(s[11], 4 * half, 4), 4)[:, :, C - 1:C].broadcast_to([P, 4, C]),
                            ALU.mult).then_inc(*done(half))
                    else:
                        ts_(chunk(s[16], 4 * half, 4), ps[:], consts[:, K_RK + h:K_RK + h + 1], None, ALU.mult).then_inc(*done(half))
                for half in range(2):
                    ps = take(2 + half)
                    if delta:
                        tt_(cut(chunk(s[17], 4 * half, 4), 4), cut(ps[:], 4),
                            gcol[:, 4 * half:4 * half + 4, 32 + h:33 + h].broadcast_to([P, 4, C]), ALU.mult).then_inc(*done(2 + half))
                    else:
                        nc.vector.tensor_copy(chunk(s[17], 4 * half, 4), ps[:]).then_inc(*done(2 + half))
                if delta:
                    for half in range(2):
                        ps = take((4, 0)[half])
                        tt_(chunk(s[12], 4 * half, 4), ps[:], chunk(s[11], 4 * half, 4), ALU.mult).then_inc(*done((4, 0)[half]))
                for half in range(2):
                    ps = take(1 + half)
                    dec = cut(chunk(s[11], 4 * half, 4), 4) if delta else rep(s[8][:, h * P:(h + 1) * P], 4)
                    tt_(cut(chunk(s[13], 4 * half, 4), 4), cut(ps[:], 4), dec, ALU.mult).then_inc(*done(1 + half))
                if delta:
                    Pm, Dm, E = s[11], s[14], s[15]

                    def even_blocks(a, lv):
                        return cut(a, 4).rearrange("p q (n two b) -> p q n two b", two=2, b=1 << lv)[:, :, :, 0, :]

                    def cut_free(a, n):
                        return a[:, :, 0].rearrange("p (q m) -> p q m", q=n)

                    for half in range(2):
                        tell(to_pe)
                        yield "invert"
                    e = every_other(chunk(E, 0, NC_), 0, 1)
                    nc.vector.tensor_copy(cut(chunk(E, 0, NC_), NC_), rep(ident, NC_)).then_inc(*n.stepped())
                    nc.vector.tensor_copy(cut(chunk(Dm, 0, NC_), NC_), rep(ident, NC_))
                    p = every_other(chunk(Pm, 0, NC_), 0, 1)
                    step(tt_(cut_free(p, NC_), cut_free(every_other(chunk(s[12], 0, NC_), 0, 1), NC_),
                             levels[:, LEVELS, :].unsqueeze(1).broadcast_to([P, NC_, P // 2]), ALU.mult))
                    step(tt_(e, e, p, ALU.subtract))
                    for half in range(2):
                        ps = take(half)
                        p, d = (every_other(chunk(a, 4 * half, 4), 0, 0) for a in (Pm, Dm))
                        tt_(cut_free(p, 4), cut_free(every_other(ps[:], 0, 0), 4),
                            levels[:, 0, :].unsqueeze(1).broadcast_to([P, 4, P // 2]), ALU.mult).then_inc(*done(half))
                        n.settle()
                        step(tt_(d, d, p, ALU.subtract))
                        nc.vector.memset(every_other(chunk(Pm, 4 * half, 4), 1, 1), 0.0).then_inc(*n.made(to_pe))
                        yield f"level {half}"
                    n.settle()
                    for lv in range(1, LEVELS):
                        for half in range(2):
                            ps = take(half)
                            mask = levels[:, lv, :].rearrange("p (n b) -> p n b", b=1 << lv)
                            tt_(even_blocks(chunk(Pm, 4 * half, 4), lv), even_blocks(ps[:], lv),
                                mask.unsqueeze(1).broadcast_to([P, 4, mask.shape[1], 1 << lv]), ALU.mult).then_inc(*done(half))
                            tell(to_pe)
                            yield "block"
                        for half in range(2):
                            b = (3, half)[half]
                            ps = take(b)
                            e = every_other(chunk(E, 4 * half, 4), lv, 1)
                            tt_(e, e, every_other(ps[:], lv, 1), ALU.subtract).then_inc(*done(b))
                            n.settle()
                            if lv < LEVELS - 1:
                                tell(to_pe)
                                yield "turn"
                        if lv < LEVELS - 1:
                            for half in range(2):
                                b = (2, 4)[half]
                                ps = take(b)
                                d = every_other(chunk(Dm, 4 * half, 4), lv, 0)
                                nc.vector.tensor_copy(d, every_other(ps[:], lv, 0)).then_inc(*done(b))
                                tell(to_pe)
                                left = chunk(Pm, 4 * half, 4).rearrange("p (n x y b) -> p n x y b", x=2, y=2, b=1 << lv)
                                nc.vector.memset(left[:, :, 1, 0, :], 0.0)
                                yield f"level {half}"
                n.settle()
                if unit:
                    v.wait_ge(stored, n.awaited(stored, 32)[1])
                nc.vector.memset(S[:, 0:P], 0.0).then_inc(*n.made(to_pe))
                yield "scan"
                for c in range(NC_):
                    if delta:
                        ps = take(0)
                        stt(resid[:], ps[:, 0:P], negbe[:, c, h:h + 1], chunk(s[17], c), ALU.mult, ALU.add).then_inc(*done(0))
                        tell(to_pe)
                        yield "residual"
                        ps = take(1)
                        nc.vector.tensor_copy(vnew[:], ps[:, 0:P]).then_inc(*done(1))
                        tell(to_pe)
                        yield "values"
                    ps = take(3)
                    gl = s[7][:, c * C + C - 1:c * C + C] if delta else consts[:, K_RG + 4 + h:K_RG + 5 + h]
                    stt(S[:, 0:P], S[:, 0:P], gl, ps[:, 0:P], ALU.mult, ALU.add).then_inc(*done(3))
                    n.settle()
                    if c < NC_ - 1:
                        tell(to_pe)
                        yield "state"
                qs, ks = q[:, SEQ:TOK], k[:, SEQ:TOK]
                sm = [small[:, j * NB:(j + 1) * NB] for j in range(12)]
                nc.vector.tensor_copy(kq[:, :, 0], ks)
                nc.vector.tensor_copy(kq[:, :, 1], qs)
                tt_(sm[0], qs, ks, ALU.mult).then_inc(*n.made(to_pe))
                yield "sample"
                ps = take(4)
                step(nc.vector.tensor_copy(small[:, 4 * NB:7 * NB], ps[:, 0:3 * NB]))
                nc.vector.tensor_copy(sm[0], ks).then_inc(*done(4))
                KS = small[:, 4 * NB:6 * NB].rearrange("p (b two) -> p b two", two=2)[:, :, 0]
                QS = small[:, 4 * NB:6 * NB].rearrange("p (b two) -> p b two", two=2)[:, :, 1]
                if delta:
                    egs, bbs = s[7][:, SEQ:TOK], s[8][:, SEQ:TOK]
                    step(tt_(sm[2], KS, egs, ALU.mult))
                    step(tt_(sm[2], vs, sm[2], ALU.subtract))
                    step(tt_(sm[1], sm[2], bbs, ALU.mult))
                    vs = sm[1]
                    step(tt_(sm[2], QS, egs, ALU.mult))
                else:
                    step(ts_(sm[2], QS, consts[:, K_RG + h:K_RG + h + 1], None, ALU.mult))
                step(tt_(sm[3], sm[6], vs, ALU.mult))
                tt_(OT[:, SEQ:TOK] if not delta else sm[7], sm[2], sm[3], ALU.add).then_inc(*n.made(to_pe))
                yield "rows"
                ps = take(4)
                step(nc.vector.tensor_copy(krow[:], ps[0:NB, 0:P]))
                nc.vector.tensor_copy(vrow[:, 0:P], ps[0:NB, P:2 * P]).then_inc(*done(4))
                n.settle()
                if delta:
                    step(nc.vector.tensor_copy(OT[:, SEQ:TOK], sm[7]))
                tell(to_act)
                sample_outer(s[13], 0)
                tell(to_pe)
                yield "output"
                SS = cut(s[9][:, 0:NB * P], NB)
                v.wait_ge(state_in, n.awaited(state_in, 16)[1])
                if delta:
                    step(tt_(SS, SS, spread(egs, P), ALU.mult))
                else:
                    step(ts_(s[9][:, 0:NB * P], s[9][:, 0:NB * P], consts[:, K_RG + h:K_RG + h + 1], None, ALU.mult))
                yield "outer"
                for half in range(2):
                    b = (3, 0)[half]
                    ps = take(b)
                    x = s[9][:, half * 512:(half + 1) * 512]
                    tt_(x, x, ps[:], ALU.add).then_inc(*done(b))
                tell(to_act)
                gain = vcol(V_GDN if delta else V_RET)
                if unit == 2 * HEADS - 1:
                    for tt in range(NT):
                        v.wait_ge(*n.awaited(to_dve))
                        o, m = third(OT, tt), MIX[:, unit, tt * TT:(tt + 1) * TT]
                        step(tt_(o, o, third(s[12], tt), ALU.mult))
                        stt(m, o, gain, m, ALU.mult, ALU.mult).then_inc(*n.made(to_act))
                        mix_split(ops[0], 0, tt - 1)
                    return
                v.wait_ge(*n.awaited(to_dve))
                step(tt_(OT[:], OT[:], s[12][:], ALU.mult))
                step(stt(MIX[:, unit, :], OT[:], gain, MIX[:, unit, :], ALU.mult, ALU.mult))

            def mixer_c(s, h, start=None):
                q, k = s[0], s[1]
                for tt in range(NT):
                    ps = take(tt)
                    nc.vector.tensor_copy(third(s[12], tt), ps[:, 0:TT]).then_inc(*done(tt))
                n.settle()
                for c in range(NC_):
                    last = ts_(chunk(s[11], c), chunk(s[12], c), gcol[:, c, h:h + 1], 0.0, ALU.add, ALU.min)
                ps = take(3)
                nc.vector.tensor_copy(small[:, 10 * NB:11 * NB], ps[:, NB:2 * NB])
                tt_(small[:, 8 * NB:9 * NB], ps[:, 0:NB], s[12][:, SEQ:TOK], ALU.add).then_inc(*done(3))
                tell(to_act)
                if start:
                    start()
                yield "start"
                v.wait_ge(*n.awaited(to_dve))
                nc.vector.tensor_copy(samp[:, 0:NB], q[:, SEQ:TOK])
                for j in range(3):
                    nc.vector.tensor_copy(samp[:, (j + 1) * NB:(j + 2) * NB], s[j + 1][:, SEQ:TOK])
                step(ts_(MIX[:, 2 * h, :], s[16][:], 1.0, None, ALU.add))
                yield "gate 0"
                v.wait_ge(*n.awaited(to_dve))
                step(ts_(MIX[:, 2 * h + 1, :], s[17][:], 1.0, None, ALU.add))
                yield "gate 1"
                step(tt_(cut(s[11][:, 0:SEQ], NC_), cut(s[11][:, 0:SEQ], NC_), rep(causal, NC_), ALU.mult))
                tt_(s[10][:], q[:], s[6][:], ALU.mult).then_inc(*n.made(to_pe))
                yield "operands"
                for half in range(2):
                    ps = take(half)
                    tt_(cut(chunk(s[16], 4 * half, 4), 4), cut(ps[:], 4),
                        cut(chunk(s[11], 4 * half, 4), 4)[:, :, C - 1:C].broadcast_to([P, 4, C]), ALU.mult).then_inc(*done(half))
                for half in range(2):
                    ps = take(2 + half)
                    nc.vector.tensor_copy(chunk(s[17], 4 * half, 4), ps[:]).then_inc(*done(2 + half))
                for half in range(2):
                    b = (4, 0)[half]
                    ps = take(b)
                    nc.vector.tensor_copy(chunk(s[13], 4 * half, 4), ps[:]).then_inc(*done(b))
                n.settle()
                for half in range(2):
                    ps = take(1 + half)
                    x = chunk(s[11], 4 * half, 4)
                    tt_(x, ps[:], x, ALU.mult).then_inc(*done(1 + half))
                n.settle()
                if h:
                    v.wait_ge(stored, n.awaited(stored, 64)[1])
                nc.vector.memset(S[:], 0.0).then_inc(*n.made(to_pe))
                yield "scan"
                for c in range(NC_):
                    ps = take(3)
                    stt(S[:], S[:], s[6][:, c * C + C - 1:c * C + C], ps[:, 0:2 * P + 1], ALU.mult, ALU.add).then_inc(*done(3))
                    n.settle()
                    if c < NC_ - 1:
                        tell(to_pe)
                        yield "state"
                ps = take(2)
                rec = small[:, 11 * NB:12 * NB]
                nc.vector.tensor_copy(rec, ps[:, 0:NC_]).then_inc(*done(2))
                n.settle()
                step(stt(rec, rec, -1.0, rec, ALU.mult, ALU.max))
                step(tt_(rec, rec, gcol[:, :, HEADS + h], ALU.max))
                nc.vector.reciprocal(rec, rec).then_inc(*n.made(to_pe))
                yield "den"
                v.wait_ge(*n.awaited(to_dve))
                for half in range(2):
                    ps = take(2 + half)
                    for x in (12, 14):
                        o = chunk(s[x], 4 * half, 4)
                        last = tt_(o, o, ps[:], ALU.mult)
                    last.then_inc(*done(2 + half))
                n.settle()
                qs, ks = samp[:, 0:NB], samp[:, NB:2 * NB]
                sm = [small[:, j * NB:(j + 1) * NB] for j in range(12)]
                n0 = vec[:, V_N0 + h * NB:V_N0 + (h + 1) * NB]
                step(tt_(sm[1], n0, qs, ALU.mult))
                tt_(sm[0], qs, ks, ALU.mult).then_inc(*n.made(to_pe))
                yield "sample"
                ps = take(4)
                step(nc.vector.tensor_copy(small[:, 4 * NB:8 * NB], ps[:, 0:4 * NB]))
                tt_(sm[0], ks, sm[8], ALU.mult).then_inc(*done(4))
                tell(to_pe)
                yield "rows"
                ws = s[6][:, SEQ:TOK]
                step(tt_(sm[2], sm[6], sm[8], ALU.mult))
                step(tt_(sm[7], sm[7], ws, ALU.mult))
                step(tt_(sm[7], sm[7], sm[2], ALU.add))
                step(stt(sm[7], sm[7], -1.0, sm[7], ALU.mult, ALU.max))
                step(tt_(sm[7], sm[7], sm[10], ALU.max))
                step(nc.vector.reciprocal(sm[7], sm[7]))
                for j in range(2):
                    step(tt_(sm[4 + j], sm[4 + j], ws, ALU.mult))
                    step(tt_(sm[9], sm[2], samp[:, (2 + j) * NB:(3 + j) * NB], ALU.mult))
                    step(tt_(sm[4 + j], sm[4 + j], sm[9], ALU.add))
                    step(tt_(s[(12, 14)[j]][:, SEQ:TOK], sm[4 + j], sm[7], ALU.mult))
                tell(to_act)
                step(tt_(n0, n0, ws, ALU.mult))
                step(tt_(n0, n0, sm[0], ALU.add))
                ps = take(4)
                step(nc.vector.tensor_copy(krow[:], ps[0:NB, 0:P]))
                nc.vector.tensor_copy(vrow[:], ps[0:NB, P:3 * P]).then_inc(*done(4))
                n.settle()
                for j in range(2):
                    sample_outer(s[13], j)
                    tell(to_pe)
                    if j == 0:
                        yield "output"
                        v.wait_ge(state_in, n.awaited(state_in, 16)[1])
                        step(tt_(ss_c[:], ss_c[:], spread(ws, 2 * P), ALU.mult))
                    yield "outer"
                    for half in range(2):
                        b = (3, 0)[half]
                        ps = take(b)
                        x = ss_c[:, 4 * half:4 * half + 4, j * P:(j + 1) * P]
                        tt_(x, x, cut(ps[:], 4), ALU.add).then_inc(*done(b))
                    n.settle()
                tell(to_act)
                if h == HEADS - 1:
                    for tt in range(NT):
                        v.wait_ge(*n.awaited(to_dve))
                        for j in range(2):
                            x, m = third(s[(12, 14)[j]], tt), MIX[:, 2 * h + j, tt * TT:(tt + 1) * TT]
                            step(stt(x, x, vcol(V_ML + j), third(s[10], tt), ALU.mult, ALU.mult))
                            last = tt_(m, m, x, ALU.mult)
                        last.then_inc(*n.made(to_act))
                        mix_split(ops[1], 1, tt - 1)
                    return
                v.wait_ge(*n.awaited(to_dve))
                for j in range(2):
                    x = s[(12, 14)[j]]
                    step(stt(x[:], x[:], vcol(V_ML + j), s[10][:], ALU.mult, ALU.mult))
                    step(tt_(MIX[:, 2 * h + j, :], MIX[:, 2 * h + j, :], x[:], ALU.mult))

            def mlp(t0, X, Y, number, gain, Xn):
                def up(t, c):
                    for tt in range(NT):
                        drain(t, tt, lambda ps, tt: tt_(T_third[:], ps, third(rbc, tt), ALU.mult))
                        v.wait_ge(proj_drained, 3 * t + tt + 1)
                        step(stt(U_third[:], T_third[:], 0.0, T_third[:], ALU.max, ALU.mult))
                        hi, lo = (y[:, c, tt * TT:(tt + 1) * TT] for y in Y)
                        step(nc.vector.tensor_copy(hi, U_third[:]))
                        tt_(lo, U_third[:], hi.bitcast(F32), ALU.subtract).then_inc(x_ready, 1)

                v.wait_ge(*n.awaited(rbc_ready))
                with n.loop(GROUPS - 1, {dve_step.name: 2 * NT * KC}) as g:
                    for c in range(KC):
                        up(t0 + 16 * g + c, c)
                    for c in range(KC):
                        for tt in range(NT):
                            hh = H[:, c, tt * TT:(tt + 1) * TT]
                            drain(t0 + 16 * g + 8 + c, tt, lambda ps, tt: tt_(hh, hh, ps, ALU.add))
                t1 = t0 + 16 * (GROUPS - 1)
                for c in range(KC):
                    up(t1 + c, c)
                v.wait_ge(x_ready, XR["hid0" if number == 2 else "hid1"] + 24 * GROUPS)
                for c in range(KC):
                    residual(t1 + 8 + c, c, c, number, gain, Xn)

            XA, XB = ops
            nc.vector.memset(eps[:, 0:1], EPS)
            nc.vector.memset(eps[:, 1:2], 1.0)
            v.wait_ge(consts_in, 32)
            for a, m in ((V_CONV, 48), (V_GDN, 4)):
                last = ts_(vec[:, a:a + m], vec[:, a:a + m], 0.5, None, ALU.mult)
            last.then_inc(setup_done, 1)
            for c in range(KC):
                v.wait_ge(h_in[c], 16)
                for tt in range(NT):
                    hi, lo = (x[:, c, tt * TT:(tt + 1) * TT] for x in XA)
                    hh, gain = H[:, c, tt * TT:(tt + 1) * TT], vcol(V_GAIN["mix_a"] + c)
                    made = n.awaited(sq_made)
                    if tt < HI_BY_ACT:
                        v.wait_ge(*made)
                    else:
                        step(ts_(hi, hh, gain, None, ALU.mult))
                    stt(lo, hh, gain, hi.bitcast(F32), ALU.mult, ALU.subtract).then_inc(x_ready, 1)
            s = slots[0]
            v.wait_ge(x_ready, 24)
            v.wait_ge(sq_made, 24)
            step(nc.vector.memset(rows_a[0:36, :], 0.0))
            v.wait_ge(*n.awaited(rbc_ready))
            for tt in range(NT):
                v.wait_ge(proj_full, tt + 1)
                step(tt_(s[12][0:HEADS, tt * TT:(tt + 1) * TT], PJ[0:HEADS, tt, 0:TT], rbc[0:HEADS, tt * TT:(tt + 1) * TT], ALU.mult))
                tt_(rows_a[32:36, tt * TT:(tt + 1) * TT], PJ[32:36, tt, 0:TT],
                    rbc[32:36, tt * TT:(tt + 1) * TT], ALU.mult).then_inc(proj_drained, 1)
            v.wait_ge(proj_drained, NT)
            first = projections(s, T_AB, 0, 4)
            a = s[12][0:HEADS, :]
            ts_(a, a, vec[0:HEADS, V_DTB:V_DTB + 1], None, ALU.add).then_inc(*n.made(to_act))
            n.settle()
            next(first)
            v.wait_ge(*n.awaited(to_dve))
            step(ts_(negea[0:HEADS, :], negea[0:HEADS, :], -1.0, None, ALU.mult))
            step(stt(a, a, 0.0, s[13][0:HEADS, :], ALU.max, ALU.add))
            step(ts_(a, a, negea[0:HEADS, :], None, ALU.mult))
            next(first)
            v.wait_ge(mask_in, 16)
            step(nc.vector.tensor_tensor_scan(rows_a[0:HEADS, :], s[11][0:HEADS, :], a, 0.0, ALU.mult, ALU.add))
            ts_(rows_a[32:36, :], rows_a[32:36, :], 0.5, 0.5, ALU.mult, ALU.add).then_inc(*n.made(to_pe))
            for _ in first:
                pass
            for half in range(2):
                ps = take(half)
                nc.vector.tensor_copy(gcol[:, 4 * half:4 * half + 4, :], cut(ps[:, 0:4 * 36], 4)).then_inc(*done(half))
            n.settle()
            tell(to_act)
            v.wait_ge(*n.awaited(to_dve))
            step(stt(negbe[:], negbe[:], -1.0, gcol[:, :, 32:36], ALU.mult, ALU.mult))
            v.wait_ge(mask_in, 32)
            for u in range(2 * HEADS):
                all_drained(T_AB + 4 * u + 3)
                tell(to_act)
                mixer = mixer_ab(s, u % HEADS, u < HEADS, u)
                if u < 2 * HEADS - 1:
                    weave(mixer, projections(s, T_AB, u + 1, 4), DELTA_FILL if u < HEADS else RETENTION_FILL)
                else:
                    out_start(0, XA)
                    weave(mixer, out_partial(s, 0, T_OUTA), RETENTION_LAST_FILL, KC - KTAIL[0])
            mix_split(XA, 0, NT - 1)
            v.wait_ge(stored, n.awaited(stored, 32)[1])
            out_rest(s, 0, T_OUTA, 1, V_GAIN["ffn0"], XB, 2)
            mlp(T_MLP0, XB, XA, 2, V_GAIN["mix_c"], XB)
            s = slots[1]
            v.wait_ge(*n.awaited(rbc_ready))
            v.wait_ge(h_spilled, 16 * KC)
            step(nc.vector.memset(rows_c[0:100, :], 0.0))
            I, F, B, Mr = (s[j][0:HEADS, :] for j in (12, 13, 14, 15))
            for tt in range(NT):
                v.wait_ge(proj_full, 3 * T_GC + tt + 1)
                step(tt_(I[:, tt * TT:(tt + 1) * TT], PJ[0:HEADS, tt, 0:TT], rbc[0:HEADS, tt * TT:(tt + 1) * TT], ALU.mult))
                tt_(F[:, tt * TT:(tt + 1) * TT], PJ[32:36, tt, 0:TT], rbc[32:36, tt * TT:(tt + 1) * TT],
                    ALU.mult).then_inc(proj_drained, 1)
            all_drained(T_GC)
            first = projections(s, T_C, 0, 6)
            step(ts_(I, I, vec[0:HEADS, V_BI:V_BI + 1], None, ALU.add))
            ts_(F, F, vec[0:HEADS, V_BF:V_BF + 1], None, ALU.add).then_inc(*n.made(to_act))
            n.settle()
            next(first)
            v.wait_ge(*n.awaited(to_dve))
            step(stt(F, F, 0.0, s[16][0:HEADS, :], ALU.min, ALU.subtract))
            v.wait_ge(mask_in, 48)
            step(nc.vector.tensor_tensor_scan(B, s[11][0:HEADS, :], F, 0.0, ALU.mult, ALU.add))
            step(nc.vector.tensor_tensor_scan(Mr[:, 0:SEQ], F[:, 0:SEQ], I[:, 0:SEQ], 0.0, ALU.add, ALU.max))
            next(first)
            m0 = vec[0:HEADS, V_M0:V_M0 + NB]
            step(tt_(Mr[:, SEQ:TOK], F[:, SEQ:TOK], m0, ALU.add))
            step(tt_(Mr[:, SEQ:TOK], Mr[:, SEQ:TOK], I[:, SEQ:TOK], ALU.max))
            step(tt_(rows_c[0:HEADS, :], B, Mr, ALU.subtract))
            r1 = rows_c[0:HEADS, :]
            next(first)
            nc.vector.tensor_copy(rows_c[32:36, 0:C], r1[:, 0:C])
            tt_(cut(rows_c[32:36, C:SEQ], NC_ - 1), cut(r1[:, C:SEQ], NC_ - 1),
                cut(Mr[:, 0:SEQ - C], NC_ - 1)[:, :, C - 1:C].broadcast_to([HEADS, NC_ - 1, C]), ALU.add)
            tt_(rows_c[32:36, SEQ:TOK], r1[:, SEQ:TOK], m0, ALU.add)
            ts_(rows_c[64:68, :], Mr, -1.0, None, ALU.mult)
            tt_(rows_c[96:100, :], I, B, ALU.subtract).then_inc(*n.made(to_pe))
            n.settle()
            tell(to_act)
            for _ in first:
                pass
            for half in range(2):
                ps = take(half)
                nc.vector.tensor_copy(gcol[:, 4 * half:4 * half + 4, HEADS:2 * HEADS], cut(ps[:, 0:400], 4)[:, :, 64:68])
                nc.vector.tensor_copy(gcol[:, 4 * half:4 * half + 4, 0:HEADS],
                                      cut(ps[:, 0:400], 4)[:, :, 96:100]).then_inc(*done(half))
            tell(to_act)
            v.wait_ge(*n.awaited(to_dve))
            v.wait_ge(stored, n.awaited(stored, 32)[1])
            for u in range(HEADS):
                all_drained(T_C + 6 * u + 5)
                tell(to_act)
                if u < HEADS - 1:
                    weave(mixer_c(s, u), projections(s, T_C, u + 1, 6), MLSTM_FILL)
                else:
                    weave(mixer_c(s, u, lambda: out_start(1, XB)), out_partial(s, 1, T_OUTC), MLSTM_LAST_FILL, KC - KTAIL[1])
            mix_split(XB, 1, NT - 1)
            v.wait_ge(stored, n.awaited(stored, 64)[1])
            out_rest(s, 1, T_OUTC, 3, V_GAIN["ffn1"], XA, 3)
            mlp(T_MLP1, XA, XB, 4, V_GAIN["final"], None)
            v.wait_ge(*n.awaited(rbc_ready))
            for c in range(KC):
                stt(H[:, c, :], H[:, c, :], vcol(V_GAIN["final"] + c), rbc[:], ALU.mult, ALU.mult).then_inc(y_done, 1)

        @block.scalar
        def _(a):
            n = Tally(a, act_step)
            act = nc.scalar.activation
            LNEXP = "natural_log_exp_and_others"

            def take(b):
                a.wait_ge(*n.awaited(full["act"][b]))
                return MB[b]

            def done(b):
                return n.made(drained["act"][b])

            def step(ins):
                ins.then_inc(*n.stepped())
                n.settle()

            def tell(sem):
                n.settle()
                a.sem_inc(*n.made(sem))

            def rsqrt_of_banks(dst, scale, sig, by_third=False):
                for tt in range(NT):
                    ps = take(tt)
                    act(third(dst, tt), ps[:, 0:TT], ACT.Ln, bias=eps[:, 0:1], scale=scale).then_inc(*done(tt))
                n.settle()
                for part in [third(dst, tt) for tt in range(NT)] if by_third else [dst[:]]:
                    act(part, part, ACT.Exp, scale=-0.5).then_inc(*n.made(sig))

            def squares(c, at, tt, number):
                hh = H[:, c, tt * TT:(tt + 1) * TT]
                if at >= 2:
                    a.wait_ge(ssq_added, 21 * number + 3 * (at - 2) + tt + 1)
                act(third(SQT if at else SSQ, tt), hh, ACT.Square).then_inc(sq_made, 1)

            def norm_of(t0, number, after=None, layer=None, high=None):
                t = t0
                for at, c in enumerate(IN_TURN if layer is None else ORDER[layer]):
                    partial = layer is not None and c in PARTIAL[layer]
                    for tt in range(NT):
                        if partial:
                            a.wait_ge(*n.awaited(h_added))
                        else:
                            a.wait_ge(proj_drained, 3 * t + tt + 1)
                        if high:
                            X, gain = high
                            act(X[:, c, tt * TT:(tt + 1) * TT], H[:, c, tt * TT:(tt + 1) * TT], ACT.Copy,
                                scale=vec[:, gain + c:gain + c + 1])
                        squares(c, at, tt, number)
                    t += not partial
                    if after:
                        after(c)
                rsqrt_of_banks(rbc, 1.0 / D_MODEL, rbc_ready)

            def store(dst, src):
                a.dma_start(dst, src).then_inc(stored, 16)

            def mix_high(layer, X):
                for c in range(KC - KTAIL[layer]):
                    act(X[0][:, c, :], MIX[:, c, :], ACT.Copy).then_inc(mix_hi, 1)

            def mix_high_last(layer, X):
                for tt in range(NT):
                    a.wait_ge(*n.awaited(to_act))
                    for c in range(KC - KTAIL[layer], KC):
                        act(X[0][:, c, tt * TT:(tt + 1) * TT], MIX[:, c, tt * TT:(tt + 1) * TT],
                            ACT.Copy).then_inc(mix_hi, 1)

            def reload(src, base, chunks):
                for c in chunks:
                    a.wait_ge(x_ready, base + (3 * c + 3 if len(chunks) > 2 else 3 * KC))
                    a.dma_start(H[:, c, :], src[c]).then_inc(h_in[c], 16)

            def mixer_ab(s, h, delta, start=None, midway=None):
                a.wait_ge(*n.awaited(to_act))
                if start:
                    start()
                if not delta or h:
                    a.wait_ge(stored, n.awaited(stored, 32)[1])
                a.dma_start(s[9][:, 0:NB * P], io["state_a" if delta else "state_b"][h]).then_inc(state_in, 16)
                def newest_tap(x):
                    w = V_CONV + 4 * (x * HEADS + h) + 3
                    return act(s[4 + x][:], s[x][:], ACT.Copy, scale=vec[:, w:w + 1])

                if delta:
                    for tt in range(NT):
                        ps = take(tt)
                        act(third(s[8], tt), ps[:, 0:TT], ACT.Copy).then_inc(*done(tt))
                act(s[16][:], s[3][:], ACT.Tanh, scale=0.5).then_inc(*n.made(to_dve))
                if delta:
                    for x in (1, 2):
                        newest_tap(x).then_inc(*n.stepped())
                    a.wait_ge(*n.awaited(to_act))
                    act(s[10][:], s[4][:], ACT.Tanh).then_inc(*n.made(to_dve))
                    tell(to_dve)
                    a.wait_ge(*n.awaited(to_act))
                    act(s[7][:], s[7][:], ACT.Exp)
                    act(s[11][:, 0:SEQ], s[11][:, 0:SEQ], ACT.Exp).then_inc(*n.made(to_dve))
                    a.wait_ge(*n.awaited(to_act))
                    act(s[10][:], s[4][:], ACT.Square).then_inc(*n.made(act_to_pe))
                    a.wait_ge(*n.awaited(to_act))
                    act(s[12][:], s[5][:], ACT.Tanh).then_inc(*n.made(to_dve))
                    a.wait_ge(*n.awaited(to_act))
                    act(s[12][:], s[5][:], ACT.Square).then_inc(*n.made(act_to_pe))
                    a.wait_ge(*n.awaited(to_act))
                    act(s[13][:], s[6][:], ACT.Tanh).then_inc(*n.made(to_dve))
                    nc.scalar.preload_act_table_set(LNEXP)
                    for sq in (10, 12):
                        rsqrt_of_banks(s[sq], 1.0, to_dve)
                    OT = s[6]
                else:
                    for x in range(2):
                        rot = s[(12, 14)[x]]
                        act(rot[0:64, :], s[x][64:128, :], ACT.Copy)
                        act(rot[64:128, :], s[x][0:64, :], ACT.Copy).then_inc(*n.made(to_dve))
                    OT = s[11]
                for c in range(NC_):
                    ps = take(2)
                    act(chunk(OT, c), ps[:, 0:C], ACT.Copy).then_inc(*done(2))
                n.settle()
                if midway:
                    midway()
                a.wait_ge(*n.awaited(to_act))
                act(s[12][:], OT[:], ACT.Square).then_inc(*n.made(act_to_pe))
                nc.scalar.preload_act_table_set(LNEXP)
                rsqrt_of_banks(s[12], 1.0 / DK, to_dve, by_third=midway is not None)
                a.wait_ge(*n.awaited(to_act))
                store(io["s_state_a" if delta else "s_state_b"][h], s[9][:, 0:NB * P])
                store(io["p_state_a" if delta else "p_state_b"][h], S[:, 0:P])

            def mixer_c(s, h, start=None, midway=None):
                a.wait_ge(*n.awaited(to_act))
                if start:
                    start()
                if h:
                    a.wait_ge(stored, n.awaited(stored, 64)[1])
                a.dma_start(ss_c[:], io["state_c"][h].rearrange("p (b v) -> p b v", b=NB)).then_inc(state_in, 16)
                for j in range(2):
                    last = act(s[16 + j][:], s[4 + j][:], ACT.Tanh, scale=0.5)
                last.then_inc(*n.made(to_dve))
                a.wait_ge(*n.awaited(to_act))
                act(s[11][:, 0:SEQ], s[11][:, 0:SEQ], ACT.Exp)
                for j in (8, 10):
                    act(small[:, j * NB:(j + 1) * NB], small[:, j * NB:(j + 1) * NB], ACT.Exp)
                for tt in range(NT):
                    ps = take(tt)
                    act(third(s[6], tt), ps[:, 0:TT], ACT.Exp).then_inc(*done(tt))
                n.settle()
                tell(to_dve)
                for c in range(NC_):
                    for j, x in enumerate((12, 14)):
                        ps = take(j)
                        act(chunk(s[x], c), ps[:, 0:C], ACT.Copy).then_inc(*done(j))
                tell(to_dve)
                if midway:
                    midway()
                a.wait_ge(*n.awaited(to_act))
                act(s[10][:], s[12][:], ACT.Square)
                act(s[11][:], s[14][:], ACT.Square).then_inc(*n.made(act_to_pe))
                nc.scalar.preload_act_table_set(LNEXP)
                rsqrt_of_banks(s[10], 1.0 / (2 * P), to_dve, by_third=midway is not None)
                a.wait_ge(*n.awaited(to_act))
                store(io["s_state_c"][h].rearrange("p (b v) -> p b v", b=NB), ss_c[:])
                store(io["p_state_c"][h], S[:, 0:2 * P])
                store(io["p_n"][h], S[:, 2 * P:2 * P + 1])
                store(io["s_n"][h], vec[:, V_N0 + h * NB:V_N0 + (h + 1) * NB])

            nc.scalar.preload_act_table_set(LNEXP)
            a.dma_start(consts[:], io["consts"]).then_inc(consts_in, 16)
            a.dma_start(vec[:], io["vec"]).then_inc(consts_in, 16)
            a.dma_start(slots[0][11][0:HEADS, :], io["scan_mask"]).then_inc(mask_in, 16)
            a.wait_ge(setup_done, 1)
            XH = ops[0][0]
            for c in range(KC):
                a.wait_ge(h_in[c], 16)
                for tt in range(NT):
                    if tt < HI_BY_ACT:
                        act(XH[:, c, tt * TT:(tt + 1) * TT], H[:, c, tt * TT:(tt + 1) * TT], ACT.Copy,
                            scale=vec[:, V_GAIN["mix_a"] + c:V_GAIN["mix_a"] + c + 1])
                    squares(c, c, tt, 0)
            nc.scalar.preload_act_table_set(LNEXP)
            rsqrt_of_banks(rbc, 1.0 / D_MODEL, rbc_ready)
            a.wait_ge(x_ready, 24)
            a.wait_ge(mask_in, 16)
            a.dma_start(levels[:], io["levels"].rearrange("p (l m) -> p l m", l=LEVELS + 1)).then_inc(mask_in, 16)
            s = slots[0]
            a.wait_ge(*n.awaited(to_act))
            t = s[13][0:HEADS, :]
            step(act(t, s[12][0:HEADS, :], ACT.Abs))
            step(act(t, t, ACT.Exp, scale=-1.0))
            act(negea[0:HEADS, :], vec[0:HEADS, V_ALOG:V_ALOG + 1], ACT.Exp)
            step(act(t, t, ACT.Ln, bias=eps[0:HEADS, 1:2]))
            act(rows_a[32:36, :], rows_a[32:36, :], ACT.Tanh, scale=0.5).then_inc(*n.made(to_dve))
            a.wait_ge(*n.awaited(to_act))
            act(negbe[:], gcol[:, :, 0:HEADS], ACT.Exp).then_inc(*n.made(to_dve))
            for u in range(2 * HEADS):
                if u == HEADS:
                    a.wait_ge(proj_drained, 3 * (T_AB + 4 * u))
                    a.dma_start(s[4][:], io["cos"]).then_inc(bconst_in, 16)
                    a.dma_start(s[5][:], io["sin"]).then_inc(bconst_in, 16)
                    a.dma_start(s[8][:, 0:8 * P], io["retention"]).then_inc(bconst_in, 16)
                if u < 2 * HEADS - 1:
                    mixer_ab(s, u % HEADS, u < HEADS)
                else:
                    mixer_ab(s, u % HEADS, False, lambda: mix_high(0, ops[0]),
                             lambda: reload(io["x"], XR["mix0"], [c for c in ORDER[0] if c < KC - KTAIL[0]]))
            a.dma_start(io["conv_rows"], convo[:].rearrange("p a b -> p (a b)")).then_inc(rows_stored, 16)
            mix_high_last(0, ops[0])
            reload(io["x"], XR["mix0"], range(KC - KTAIL[0], KC))
            norm_of(T_OUTA + 5, 1, layer=0, high=(ops[1][0], V_GAIN["ffn0"]))

            def spill(c):
                a.dma_start(io["h_spill"][c], H[:, c, :]).then_inc(h_spilled, 16)

            norm_of(T_MLP0 + 16 * (GROUPS - 1) + 8, 2, spill)
            s = slots[1]
            a.dma_start(s[11][0:HEADS, :], io["scan_mask"]).then_inc(mask_in, 16)
            a.wait_ge(*n.awaited(to_act))
            t = s[16][0:HEADS, :]
            step(act(t, s[13][0:HEADS, :], ACT.Abs))
            step(act(t, t, ACT.Exp, scale=-1.0))
            act(t, t, ACT.Ln, bias=eps[0:HEADS, 1:2]).then_inc(*n.made(to_dve))
            a.wait_ge(*n.awaited(to_act))
            store(io["p_m"], s[15][0:HEADS, SEQ - 1:SEQ])
            store(io["s_m"], s[15][0:HEADS, SEQ:TOK])
            n.awaited(stored, 64)
            a.wait_ge(*n.awaited(to_act))
            act(gcol[:, :, HEADS:2 * HEADS], gcol[:, :, HEADS:2 * HEADS], ACT.Exp).then_inc(*n.made(to_dve))
            for u in range(HEADS):
                if u < HEADS - 1:
                    mixer_c(s, u)
                else:
                    mixer_c(s, u, lambda: mix_high(1, ops[1]),
                            lambda: reload(io["h_spill"], XR["mix1"], [c for c in ORDER[1] if c < KC - KTAIL[1]]))
            mix_high_last(1, ops[1])
            reload(io["h_spill"], XR["mix1"], range(KC - KTAIL[1], KC))
            norm_of(T_OUTC + 5, 3, layer=1, high=(ops[0][0], V_GAIN["ffn1"]))
            norm_of(T_MLP1 + 16 * (GROUPS - 1) + 8, 4)
            for c in range(KC):
                a.wait_ge(y_done, c + 1)
                a.dma_start(io["y"][c], H[:, c, :]).then_inc(stored, 16)
            a.wait_ge(stored, 16 * (2 * 2 * HEADS + 2 + 4 * HEADS + KC))
            a.wait_ge(rows_stored, 16)
            a.wait_ge(h_spilled, 16 * KC)


def shape_constants():
    f = np.float32
    i = np.arange(P)
    consts = np.zeros((P, K_ALL), f)
    consts[:, K_ID:K_ID + P] = np.eye(P)
    consts[:, K_ONE:K_ONE + P] = 1
    consts[:, K_CAUS:K_CAUS + P] = i[:, None] <= i[None, :]
    lg = np.log1p(-np.exp2(-5.0 - np.arange(HEADS, dtype=np.float64)))
    consts[:, K_RG:K_RG + 4] = np.exp(lg)
    consts[:, K_RG + 4:K_RG + 8] = np.exp(C * lg)
    consts[:, K_RK:K_RK + 4] = np.exp(lg[None, :] * (C - 1 - i)[:, None])
    levels = np.zeros((P, LEVELS + 1, P // 2), f)
    for lv in range(LEVELS):
        b = 1 << lv
        even = i[i // b % 2 == 0]
        levels[:, lv, :] = (i[:, None] // (2 * b) == even[None, :] // (2 * b)) & (i[:, None] // b % 2 == 1)
    levels[:, LEVELS, :] = i[:, None] == i[None, ::2]
    ret = np.zeros((P, 2, HEADS, P), f)
    diff = (i[None, :] - i[:, None])
    for h in range(HEADS):
        ret[:, 0, h] = np.where(diff >= 0, np.exp(lg[h] * np.maximum(diff, 0)), 0)
        ret[:, 1, h] = np.exp(lg[h] * (i + 1))[None, :]
    half = DK // 2
    inv = (f(ROPE_BASE) ** (-np.arange(half, dtype=f) / f(half))).astype(f)
    pos = np.concatenate([np.arange(SEQ), np.full(NB, PAST_LEN)]).astype(f)
    ang = (inv[:, None] * pos[None, :]).astype(f).astype(np.float64)
    cos = np.concatenate([np.cos(ang)] * 2).astype(f)
    sin = np.concatenate([-np.sin(ang), np.sin(ang)]).astype(f)
    mask = np.ones((HEADS, TOK), f)
    mask[:, 0:SEQ:C] = 0
    mask[:, SEQ:] = 0
    return {"consts": consts, "levels": levels.reshape(P, -1), "retention": ret.reshape(P, -1),
            "cos": cos, "sin": sin, "scan_mask": mask}


def kernel(x_prompt, x_sample, state_conv_a, state_delta_a, state_ret_b, state_mlstm_C, state_mlstm_n, state_mlstm_m,
           norm_mix_a, w_in_a, w_conv_a, a_log, dt_bias, gdn_gain, ret_gain, w_out_a,
           norm_mix_c, w_in_c, b_gate_c, mlstm_gain, w_out_c, norm_ffn, w_up, w_down, final_gain):
    import concourse.bacc as bacc
    from concourse.bass_utils import run_bass_kernel_spmd

    def arr(a):
        return np.asarray(a)

    f = np.float32

    def tiles_of(w, rows, cols):
        w = arr(w)[rows:rows + D_MODEL]
        return [w[:, c:c + P].reshape(KC, P, P).transpose(1, 0, 2) for c in cols]

    def gate_tile(w, first, second):
        t = np.zeros((D_MODEL, P), f)
        t[:, 0:HEADS] = arr(w)[:, first:first + HEADS]
        t[:, 32:32 + HEADS] = arr(w)[:, second:second + HEADS]
        return t.reshape(KC, P, P).transpose(1, 0, 2)

    def mlp_tiles(layer):
        out = []
        for g in range(GROUPS):
            out += tiles_of(w_up[layer], 0, range(g * D_MODEL, (g + 1) * D_MODEL, P))
            out += tiles_of(w_down[layer], g * D_MODEL, range(0, D_MODEL, P))
        return out

    def out_tiles(w, layer):
        tail = np.zeros((P, KC, P), f)
        for k in range(KTAIL[layer]):
            for j, c in enumerate(PARTIAL[layer]):
                r = (KC - KTAIL[layer] + k) * P
                tail[:, 4 * k + j] = w[r:r + P, c * P:(c + 1) * P]
        full = [c for c in ORDER[layer] if c not in PARTIAL[layer]]
        return [tail] + tiles_of(w, 0, [c * P for c in (*PARTIAL[layer], *full)])

    wa, wc = arr(w_in_a)[0], arr(w_in_c)[0]
    tiles = [gate_tile(wa, 1536, 1540)]
    for h in range(HEADS):
        tiles += tiles_of(wa, 0, [1544 + h * P, h * P, 512 + h * P, 1024 + h * P])
    for h in range(HEADS):
        tiles += tiles_of(wa, 0, [3592 + h * P, 2056 + h * P, 2568 + h * P, 3080 + h * P])
    tiles += out_tiles(arr(w_out_a)[0], 0) + mlp_tiles(0)
    tiles += [gate_tile(wc, 3072, 3076)]
    for h in range(HEADS):
        tiles += tiles_of(wc, 0, [2048 + 2 * h * P, 2048 + (2 * h + 1) * P, 1024 + 2 * h * P, 1024 + (2 * h + 1) * P,
                                  h * P, 512 + h * P])
    tiles += out_tiles(arr(w_out_c)[0], 1) + mlp_tiles(1)
    assert len(tiles) == TILES
    w_all = np.stack(tiles).reshape(TILES, P, KC * P)

    vec = np.zeros((P, V_ALL), f)
    for name, a in (("mix_a", arr(norm_mix_a)[0]), ("ffn0", arr(norm_ffn)[0]), ("mix_c", arr(norm_mix_c)[0]),
                    ("ffn1", arr(norm_ffn)[1]), ("final", arr(final_gain))):
        vec[:, V_GAIN[name]:V_GAIN[name] + KC] = a.reshape(KC, P).T
    vec[:, V_GDN] = arr(gdn_gain)[0]
    vec[:, V_RET] = arr(ret_gain)[0]
    vec[:, V_ML:V_ML + 2] = arr(mlstm_gain)[0].reshape(2, P).T
    vec[0:HEADS, V_DTB] = arr(dt_bias)[0]
    vec[0:HEADS, V_ALOG] = arr(a_log)[0]
    vec[0:HEADS, V_BI] = arr(b_gate_c)[0, 0:HEADS]
    vec[0:HEADS, V_BF] = arr(b_gate_c)[0, HEADS:]
    vec[:, V_CONV:V_CONV + 48] = arr(w_conv_a)[0].reshape(CONV_W, 12, P).transpose(2, 1, 0).reshape(P, 48)
    vec[0:HEADS, V_M0:V_M0 + NB] = arr(state_mlstm_m)[0].T
    vec[:, V_N0:V_N0 + HEADS * NB] = arr(state_mlstm_n)[0].transpose(2, 1, 0).reshape(P, HEADS * NB)
    vec[:, V_HIST:] = arr(state_conv_a)[0].reshape(NB, 3, 12, P).transpose(3, 2, 1, 0).reshape(P, -1)

    x = np.concatenate([arr(x_prompt)[0], arr(x_sample)[:, 0]]).T.reshape(KC, P, TOK)

    def by_head(st):
        return arr(st)[0].transpose(1, 2, 0, 3).reshape(HEADS, P, -1)

    ins = {"w_all": w_all, "vec": vec, "x": x, "state_a": by_head(state_delta_a), "state_b": by_head(state_ret_b),
           "state_c": by_head(state_mlstm_C), **shape_constants()}
    ins = {k: np.ascontiguousarray(a) for k, a in ins.items()}
    outs = {"y": (KC, P, TOK), "conv_rows": (P, 12 * (3 + 3 * NB)),
            "p_state_a": (HEADS, P, P), "p_state_b": (HEADS, P, P), "p_state_c": (HEADS, P, 2 * P),
            "p_n": (HEADS, P, 1), "p_m": (HEADS, 1),
            "s_state_a": (HEADS, P, NB * P), "s_state_b": (HEADS, P, NB * P), "s_state_c": (HEADS, P, NB * 2 * P),
            "s_n": (HEADS, P, NB), "s_m": (HEADS, NB)}

    nc = bacc.Bacc("TRN2", target_bir_lowering=False, num_devices=1)
    io = {k: nc.dram_tensor(k, a.shape, F32, kind="ExternalInput").ap() for k, a in ins.items()}
    io.update({k: nc.dram_tensor(k, s, F32, kind="ExternalOutput").ap() for k, s in outs.items()})
    io["h_spill"] = nc.dram_tensor("h_spill", (KC, P, TOK), F32, kind="Internal").ap()
    build(nc, io)
    r = run_bass_kernel_spmd(nc, [ins], core_ids=[0]).results[0]

    y = r["y"].reshape(D_MODEL, TOK).T
    conv = r["conv_rows"].reshape(P, 12, 3 + 3 * NB)
    p_conv = conv[:, :, 0:3].transpose(2, 1, 0).reshape(1, 1, 3, 12 * P)
    s_conv = conv[:, :, 3:].reshape(P, 12, 3, NB).transpose(3, 2, 1, 0).reshape(1, NB, 3, 12 * P)

    def samples(a, v):
        return np.ascontiguousarray(a.reshape(HEADS, P, NB, v).transpose(2, 0, 1, 3))[None]

    out = (y[0:SEQ][None], y[SEQ:][:, None], p_conv, r["p_state_a"][None, None], r["p_state_b"][None, None],
           r["p_state_c"][None, None], r["p_n"].reshape(1, 1, HEADS, P), r["p_m"].reshape(1, 1, HEADS),
           s_conv, samples(r["s_state_a"], P), samples(r["s_state_b"], P), samples(r["s_state_c"], 2 * P),
           np.ascontiguousarray(r["s_n"].transpose(2, 0, 1))[None], np.ascontiguousarray(r["s_m"].T)[None])
    return tuple(np.ascontiguousarray(o) for o in out)
```
